# Optimizing a Trainium2 kernel written in Bass

```python
import jax, jax.numpy as jnp
from jax import lax
import numpy as np

D_MODEL = 1024
BATCH = 1
SEQ = 1024
DEPTH = 1

D_HEAD = 64
N_HEADS_TOTAL = D_MODEL // D_HEAD
D_MIX = N_HEADS_TOTAL * D_HEAD
N_HEADS_DSA = N_HEADS_TOTAL // 2
N_HEADS_FOX = N_HEADS_TOTAL - N_HEADS_DSA
N_IDX_HEADS = 4
D_IDX = 64
TOP_K_MAX = 256
ROPE_THETA = 500000.0
ROT_DIM = D_HEAD // 4
ROT_DIM_IDX = D_IDX // 4
D_FF = ((8 * D_MODEL // 3 + 255) // 256) * 256
BLOCK_Q_FOX = 128
BLOCK_Q_DSA = 64
N_MOD = 6
RMS_EPS = 1e-6

SPLIT_SIZES = (
    N_HEADS_DSA * D_HEAD,
    N_HEADS_DSA * D_HEAD,
    N_HEADS_DSA * D_HEAD,
    N_IDX_HEADS * D_IDX,
    D_IDX,
    N_IDX_HEADS,
    N_HEADS_FOX * D_HEAD,
    N_HEADS_FOX * D_HEAD,
    N_HEADS_FOX * D_HEAD,
    N_HEADS_FOX,
)
D_IN = int(sum(SPLIT_SIZES))
SPLIT_POINTS = [int(v) for v in np.cumsum(SPLIT_SIZES)[:-1]]

kernel_name = "hymba_dsa_fox_adaln_block"

def rms_norm(x, g):
    xf = x.astype(jnp.float32)
    y = xf * lax.rsqrt(jnp.mean(xf * xf, axis=-1, keepdims=True) + RMS_EPS)
    return (y * g.astype(jnp.float32)).astype(x.dtype)

def modulate(h, shift, scale):
    return h * (1 + scale[:, None, :]) + shift[:, None, :]

def split_heads(a, n):
    return a.reshape(a.shape[0], a.shape[1], n, -1)

def rope_partial(x, positions, rot_dim):
    half = rot_dim // 2
    inv_freq = ROPE_THETA ** (-jnp.arange(0, rot_dim, 2, dtype=jnp.float32) / rot_dim)
    ang = positions.astype(jnp.float32)[..., None] * inv_freq
    cos = jnp.cos(ang)[:, :, None, :]
    sin = jnp.sin(ang)[:, :, None, :]
    xf = x.astype(jnp.float32)
    x1, x2, rest = xf[..., :half], xf[..., half:rot_dim], xf[..., rot_dim:]
    out = jnp.concatenate([x1 * cos - x2 * sin, x2 * cos + x1 * sin, rest], axis=-1)
    return out.astype(x.dtype)

def to_blocks(a, bq):
    b, s = a.shape[0], a.shape[1]
    return a.reshape(b, s // bq, bq, *a.shape[2:]).swapaxes(0, 1)

def from_blocks(a):
    a = a.swapaxes(0, 1)
    return a.reshape(a.shape[0], a.shape[1] * a.shape[2], *a.shape[3:])

def dsa_attention(q, k, v, iq, ik, iw, k_top):
    s_len = q.shape[1]
    scale = D_HEAD ** -0.5
    idx_scale = D_IDX ** -0.5
    key_pos = jnp.arange(s_len)
    ik32 = ik.astype(jnp.float32)

    def one_block(args):
        qb, iqb, iwb, qpos = args
        dots = jnp.einsum('bqhd,bsd->bqhs', iqb.astype(jnp.float32), ik32) * idx_scale
        score = jnp.einsum('bqhs,bqh->bqs', jax.nn.relu(dots), iwb.astype(jnp.float32))
        causal = key_pos[None, :] <= qpos[:, None]
        score = jnp.where(causal[None], score, -jnp.inf)
        _, idx = lax.top_k(score, k_top)
        valid = idx <= qpos[None, :, None]
        k_sel = jax.vmap(lambda kk, ii: kk[ii])(k, idx)
        v_sel = jax.vmap(lambda vv, ii: vv[ii])(v, idx)
        logits = jnp.einsum('bqhd,bqkhd->bhqk', qb, k_sel).astype(jnp.float32) * scale
        logits = jnp.where(valid[:, None], logits, -jnp.inf)
        p = jax.nn.softmax(logits, axis=-1).astype(v.dtype)
        return jnp.einsum('bhqk,bqkhd->bqhd', p, v_sel)

    qpos = jnp.arange(s_len).reshape(s_len // BLOCK_Q_DSA, BLOCK_Q_DSA)
    out = lax.map(one_block, (to_blocks(q, BLOCK_Q_DSA), to_blocks(iq, BLOCK_Q_DSA),
                              to_blocks(iw, BLOCK_Q_DSA), qpos))
    return from_blocks(out)

def fox_attention(q, k, v, log_f):
    s_len = q.shape[1]
    scale = D_HEAD ** -0.5
    cum = jnp.cumsum(log_f, axis=1)
    cum_keys = cum.transpose(0, 2, 1)
    key_pos = jnp.arange(s_len)

    def one_block(args):
        qb, cq, qpos = args
        logits = jnp.einsum('bqhd,bshd->bhqs', qb, k).astype(jnp.float32) * scale
        bias = cq.transpose(0, 2, 1)[..., :, None] - cum_keys[..., None, :]
        causal = key_pos[None, :] <= qpos[:, None]
        logits = jnp.where(causal[None, None], logits + bias, -jnp.inf)
        p = jax.nn.softmax(logits, axis=-1).astype(v.dtype)
        return jnp.einsum('bhqs,bshd->bqhd', p, v)

    qpos = jnp.arange(s_len).reshape(s_len // BLOCK_Q_FOX, BLOCK_Q_FOX)
    out = lax.map(one_block, (to_blocks(q, BLOCK_Q_FOX), to_blocks(cum, BLOCK_Q_FOX), qpos))
    return from_blocks(out)

def hybrid_mixer(h, positions, w_in, b_forget, dsa_norm_g, fox_norm_g, w_out, k_top):
    b, s, _ = h.shape
    proj = h @ w_in
    q_d, k_d, v_d, iq, ik, iw, q_f, k_f, v_f, f_logit = jnp.split(proj, SPLIT_POINTS, axis=-1)
    q_d = rope_partial(split_heads(q_d, N_HEADS_DSA), positions, ROT_DIM)
    k_d = rope_partial(split_heads(k_d, N_HEADS_DSA), positions, ROT_DIM)
    v_d = split_heads(v_d, N_HEADS_DSA)
    iq = rope_partial(split_heads(iq, N_IDX_HEADS), positions, ROT_DIM_IDX)
    ik = rope_partial(ik[:, :, None, :], positions, ROT_DIM_IDX)[:, :, 0, :]
    iw = iw * (N_IDX_HEADS ** -0.5)
    o_d = dsa_attention(q_d, k_d, v_d, iq, ik, iw, k_top).reshape(b, s, -1)
    log_f = jax.nn.log_sigmoid((f_logit + b_forget).astype(jnp.float32))
    o_f = fox_attention(split_heads(q_f, N_HEADS_FOX), split_heads(k_f, N_HEADS_FOX),
                        split_heads(v_f, N_HEADS_FOX), log_f).reshape(b, s, -1)
    y = jnp.concatenate([rms_norm(o_d, dsa_norm_g), rms_norm(o_f, fox_norm_g)], axis=-1)
    return y @ w_out

def swiglu(h, w_gate, w_up, w_down):
    return (jax.nn.silu(h @ w_gate) * (h @ w_up)) @ w_down

def setup_inputs(seed: int = 0) -> dict:
    key = jax.random.key(seed)
    ks = jax.random.split(key, 16)
    f32 = jnp.float32
    nrm = lambda k, shape, s: jax.random.normal(k, shape, f32) * s
    x = jax.random.normal(ks[0], (BATCH, SEQ, D_MODEL), f32)
    c = jax.random.normal(ks[1], (BATCH, D_MODEL), f32)
    offset = jax.random.randint(ks[2], (BATCH, 1), 0, 1024, dtype=jnp.int32)
    positions = (offset + jnp.arange(SEQ, dtype=jnp.int32)[None, :]).astype(jnp.int32)
    return {
        "x": x,
        "c": c,
        "positions": positions,
        "ada_w": nrm(ks[3], (DEPTH, D_MODEL, N_MOD * D_MODEL), 0.5 * D_MODEL ** -0.5),
        "ada_b": nrm(ks[4], (DEPTH, N_MOD * D_MODEL), 0.02),
        "norm_attn_g": 1.0 + nrm(ks[5], (DEPTH, D_MODEL), 0.02),
        "w_in": nrm(ks[6], (DEPTH, D_MODEL, D_IN), D_MODEL ** -0.5),
        "b_forget": 2.0 + nrm(ks[7], (DEPTH, N_HEADS_FOX), 0.5),
        "dsa_norm_g": 1.0 + nrm(ks[8], (DEPTH, N_HEADS_DSA * D_HEAD), 0.02),
        "fox_norm_g": 1.0 + nrm(ks[9], (DEPTH, N_HEADS_FOX * D_HEAD), 0.02),
        "w_out": nrm(ks[10], (DEPTH, D_MIX, D_MODEL), D_MIX ** -0.5),
        "norm_ffn_g": 1.0 + nrm(ks[11], (DEPTH, D_MODEL), 0.02),
        "w_gate": nrm(ks[12], (DEPTH, D_MODEL, D_FF), D_MODEL ** -0.5),
        "w_up": nrm(ks[13], (DEPTH, D_MODEL, D_FF), D_MODEL ** -0.5),
        "w_down": nrm(ks[14], (DEPTH, D_FF, D_MODEL), D_FF ** -0.5),
        "final_norm_g": 1.0 + nrm(ks[15], (D_MODEL,), 0.02),
    }

def reference(x, c, positions, ada_w, ada_b, norm_attn_g, w_in, b_forget, dsa_norm_g,
              fox_norm_g, w_out, norm_ffn_g, w_gate, w_up, w_down, final_norm_g):
    s_len = x.shape[1]
    k_top = min(TOP_K_MAX, s_len // 4)
    c_act = jax.nn.silu(c)
    for l in range(DEPTH):
        mod = c_act @ ada_w[l] + ada_b[l]
        sh1, sc1, g1, sh2, sc2, g2 = jnp.split(mod, N_MOD, axis=-1)
        h = modulate(rms_norm(x, norm_attn_g[l]), sh1, sc1)
        x = x + g1[:, None, :] * hybrid_mixer(h, positions, w_in[l], b_forget[l], dsa_norm_g[l],
                                              fox_norm_g[l], w_out[l], k_top)
        h = modulate(rms_norm(x, norm_ffn_g[l]), sh2, sc2)
        x = x + g2[:, None, :] * swiglu(h, w_gate[l], w_up[l], w_down[l])
    return rms_norm(x, final_norm_g)


_drawn_inputs = setup_inputs


def setup_inputs(seed=0):
    import zlib

    import numpy as np

    out = dict(_drawn_inputs(seed))
    spreads = {}
    factors = {'norm_attn_g': 4.594,
     'dsa_norm_g': 8.0,
     'fox_norm_g': 8.0,
     'norm_ffn_g': 8.0,
     'final_norm_g': 2.867}
    for name, (base, spread) in spreads.items():
        noise = np.random.default_rng([zlib.crc32(name.encode()), seed]).standard_normal(out[name].shape)
        drawn = base * np.exp(spread * noise) if base else spread * noise
        out[name] = __import__('jax').numpy.asarray(drawn.astype(out[name].dtype))
    for name, factor in factors.items():
        out[name] = (out[name] * factor).astype(out[name].dtype)
    return out
```

```python
from contextlib import ExitStack

import numpy as np
import concourse.bass as bass
from concourse import mybir

F32 = mybir.dt.float32
F32R = mybir.dt.float32r
I32 = mybir.dt.int32
ALU = mybir.AluOpType
ACT = mybir.ActivationFunctionType

P = 128
SEQ = 1024
D = 1024
TT = SEQ // P
KT = D // P
DH = 64
NH = 8
IH = 4
ROT = DH // 4
HALF = ROT // 2
TOPK = min(256, SEQ // 4)
THETA = 500000.0
EPS = 1e-6
DFF = 2816
FT = DFF // P
FI = FT // 2
BANK = 512
GW = NH * DH
IDXW = IH * DH + DH + IH + NH
COL_IDX = 3 * GW
COL_FOX = COL_IDX + IH * DH + DH + IH
COL_F = COL_FOX + 3 * GW
BIG = 1e30
TAKEN = -3e38
SOFT = DH ** -0.5
CHUNK_COL = [COL_IDX, COL_FOX, COL_FOX + GW, COL_FOX + 2 * GW, 0, GW, 2 * GW]
NC = len(CHUNK_COL)
PIECES = 4
N_PROJ = NC * PIECES
N_OUT = KT
N_FFN0 = N_PROJ + N_OUT
FIRST_TOPK = TOPK // P

UNITS = 2 * NH * TT


def sel_off(t):
    return P * t * (t + 1) // 2


def proj_order():
    order = [("tile", 0, t) for t in range(TT)]
    between = {(1, m): ("item", m) for m in range(IH + 1)}
    slots = [(1, 5), (1, 6), (1, 7), (2, 0), (2, 1), (2, 2)]
    between.update({slot: ("score", FIRST_TOPK + i) for i, slot in enumerate(slots)})
    between[(2, 4)] = ("forget",)
    for ch in range(1, NC):
        for t in range(TT):
            order.append(("tile", ch, t))
            if (ch, t) in between:
                order.append(between[(ch, t)])
    return order


PROJ_ORDER = proj_order()
RMAGIC = 1.5 * 2.0 ** 23
PI_IN = 3.1415925
INV_FREQ = np.float32(THETA) ** (-np.arange(0, ROT, 2, dtype=np.float32) / ROT)
TWO_PI_A = 6.28125
TWO_PI_B = float(np.float32(round((2 * np.pi - 6.28125) * 2 ** 20) / 2 ** 20))
TWO_PI_C = float(2 * np.pi - 6.28125 - round((2 * np.pi - 6.28125) * 2 ** 20) / 2 ** 20)
ROPE_STEPS = 19
EARLY_ROUNDS = 152


def halves(n):
    return [(b, min(BANK, n - b)) for b in range(0, n, BANK)]


def transposes_plan():
    order = [("P", 0, part) for part in range(4)]
    for s in range(UNITS + 2):
        hd, t = divmod(s, TT)
        if s < UNITS and 1 <= t <= 4 and hd + 1 < 2 * NH:
            order.append(("P", hd + 1, t - 1))
        if s >= 2:
            order += [("T", s - 2, b) for b in range(len(halves(P * ((s - 2) % TT + 1))))]
    return order


def build(nc, x, c, positions, ada_w, ada_b, norm_attn_g, w_in, b_forget, dsa_norm_g, fox_norm_g,
          w_out, norm_ffn_g, w_gate, w_up, w_down, final_norm_g, out):
    x, c, positions, out = x[0], c[0], positions[0], out[0]
    ada_w, ada_b, w_in, w_out = ada_w[0], ada_b[0], w_in[0], w_out[0]
    w_gate, w_up, w_down = w_gate[0], w_up[0], w_down[0]
    qkv = nc.dram_tensor("qkv_scratch", (NC - 1, SEQ, GW), F32, kind="Internal").ap()
    cum_dram = nc.dram_tensor("cum_scratch", (NH, SEQ), F32, kind="Internal").ap()

    plan = transposes_plan()
    group_no = {g: n for n, g in enumerate(plan)}
    key_groups = [n for n, g in enumerate(plan) if g[0] == "P" and g[2] >= 2]

    with ExitStack() as ctx:
        def sem(name):
            return ctx.enter_context(nc.semaphore(name))

        def alloc(stack, name, shape, dt=F32):
            return stack.enter_context(nc.sbuf_tensor(name, shape, dt))

        ident = alloc(ctx, "ident", [P, P])
        ones = alloc(ctx, "ones", [P, P])
        posi = alloc(ctx, "posi", [P, TT], I32)
        posf = alloc(ctx, "posf", [P, TT])
        ccol = alloc(ctx, "ccol", [P, KT])
        cact = alloc(ctx, "cact", [P, KT])
        gains = alloc(ctx, "gains", [P, 3, KT])
        scaleA = alloc(ctx, "scaleA", [P, 2, KT])
        shiftB = alloc(ctx, "shiftB", [P, 2, KT])
        epsc = alloc(ctx, "epsc", [P, 1])
        stat = alloc(ctx, "stat", [P, 5, 16])
        rstd = alloc(ctx, "rstd", [P, 5, 16])
        bfor = alloc(ctx, "bfor", [P, NH])
        fg = alloc(ctx, "fg", [P, 4, NH * TT])
        rp = fg
        m8 = alloc(ctx, "m8", [P, 2, 8])

        with ExitStack() as s:
            hh = alloc(s, "hh", [P, KT, SEQ], F32R)
            hl = alloc(s, "hl", [P, KT, SEQ], F32R)
            with ExitStack() as s2:
                alloc(s2, "skip4", [P, 4, 2, D])
                xs = alloc(s2, "xs", [P, TT, D])
            wh = alloc(s, "wh", [P, 4, 2, 2 * BANK], F32R)
            wl = alloc(s, "wl", [P, 4, 2, 2 * BANK], F32R)
            sel = alloc(s, "sel", [P, sel_off(TT)])
            tri = alloc(s, "tri", [P, P])
            causal = alloc(s, "causal", [P, P])
            cosT = alloc(s, "cosT", [P, TT, HALF])
            sinT = alloc(s, "sinT", [P, TT, HALF])
            cumq = alloc(s, "cumq", [P, NH * TT])
            ncumq = alloc(s, "ncumq", [P, NH * TT])
            raw = alloc(s, "raw", [P, 2, D])
            stage = alloc(s, "stage", [P, 2, BANK])
            with ExitStack() as s2:
                acc1 = alloc(s2, "acc1", [P, 2 * D])
                ada1 = alloc(s2, "ada1", [P, 3, 2 * D])
                hf1 = alloc(s2, "hf1", [P, 2, BANK])
            idxn = alloc(s, "idxn", [P, TT, IDXW])
            ixs = alloc(s, "ixs", [P, 2, TT, 2, DH])
            pre = alloc(s, "pre", [P, NH, TT])
            cumT = alloc(s, "cumT", [NH * TT, P])
            iws = alloc(s, "iws", [P, TT, IH])
            qti = alloc(s, "qti", [P, IH, SEQ], F32R)
            with ExitStack() as s2:
                rot = alloc(s2, "rot", [P, 4, TT * (IH + 1) * HALF])
            kai = alloc(s, "kai", [P, SEQ], F32R)
            kbi = alloc(s, "kbi", [P, SEQ], F32R)
        with ExitStack() as s:
            O = alloc(s, "O", [P, TT, D])
            g1b = alloc(s, "g1b", [P, D])
            g2b = alloc(s, "g2b", [P, D])
            QT = alloc(s, "QT", [P, 2, SEQ], F32R)
            KA = alloc(s, "KA", [P, 2, SEQ], F32R)
            KB = alloc(s, "KB", [P, 2, SEQ], F32R)
            LP = alloc(s, "LP", [P, 3, SEQ])
            PT = alloc(s, "PT", [P, 2, SEQ])
            bt = alloc(s, "bt", [P, 2, SEQ])
            ckb = alloc(s, "ckb", [P, 2, SEQ])
            qs = alloc(s, "qs", [P, TT, 2, DH])
            kd = alloc(s, "kd", [P, TT, 2, DH])
            mod23 = alloc(s, "mod23", [P, 2, D])
            adar = alloc(s, "adar", [P, 2, D])
            adat = alloc(s, "adat", [P, D])
            alloc(s, "kept_sel", [P, sel_off(TT) + 2 * P + 2 * TT * HALF + 2 * NH * TT])
            Vn = alloc(s, "Vn", [P, 2, TT, 4 * DH])
            Qn = alloc(s, "Qn", [P, 2, TT, 4 * DH])
            Kn = alloc(s, "Kn", [P, 2, TT, 4 * DH])
            nmin = alloc(s, "nmin", [P, UNITS])
            sums = alloc(s, "sums", [P, UNITS])
            rinv = alloc(s, "rinv", [P, UNITS])
        with ExitStack() as s:
            alloc(s, "kept", [P, TT + 2, D])
            yh = alloc(s, "yh", [P, KT, SEQ], F32R)
            yl = alloc(s, "yl", [P, KT, SEQ], F32R)
            tmp = alloc(s, "tmp", [P, 2, BANK])
            with ExitStack() as s2:
                xr = alloc(s2, "xr", [P, 2, D])
            sil = alloc(s, "sil", [P, 2, BANK])
            gf = alloc(s, "gf", [P, 2, BANK])
            raw2 = alloc(s, "raw2", [P, 2, D])
            vh = alloc(s, "vh", [P, 6, D], F32R)
            vl = alloc(s, "vl", [P, 6, D], F32R)
            with ExitStack() as s2:
                vh2 = alloc(s2, "vh2", [P, 2, D], F32R)
                vl2 = alloc(s2, "vl2", [P, 2, D], F32R)
                hf2 = alloc(s2, "hf2", [P, 2, BANK])
            guh = alloc(s, "guh", [P, 2, 2, SEQ], F32R)
            gul = alloc(s, "gul", [P, 2, 2, SEQ], F32R)

        def wsl(n):
            return (wh if n % 8 < 4 else wl)[:, n % 4, 0, :], (wh if n % 8 < 4 else wl)[:, n % 4, 1, :]

        def osl(k):
            return (vh[:, k, :], vl[:, k, :]) if k < 6 else (vh2[:, k - 6, :], vl2[:, k - 6, :])

        PS = ctx.enter_context(nc.psum_tensor("PS", [P, 8, BANK], F32))

        small_in = sem("small_in")
        x_in = [sem(f"x_in{t}") for t in range(TT)]
        bias1_in = sem("bias1_in")
        ada_in = [sem(f"ada_in{i}") for i in range(3)]
        raw_in = [sem(f"raw_in{i}") for i in range(2)]
        stage_out = [sem(f"stage_out{i}") for i in range(2)]
        cum_out = sem("cum_out")
        qkv_in = [sem(f"qkv_in{i}") for i in range(2)]
        ckb_in = [sem(f"ckb_in{i}") for i in range(2)]
        mod_bias_in = sem("mod_bias_in")
        mod_in = [sem(f"mod_in{i}") for i in range(2)]
        xr_in = [sem(f"xr_in{i}") for i in range(2)]
        fgain_in = sem("fgain_in")
        out_done = sem("out_done")
        const_ok = sem("const_ok")
        const_st = sem("const_st")
        cact_ok = sem("cact_ok")
        pos_ok = sem("pos_ok")
        rope_st = sem("rope_st")
        rope_sin = sem("rope_sin")
        ssq_ok = sem("ssq_ok")
        root_ok = sem("root_ok")
        rstd_ok = sem("rstd_ok")
        xn_ok = sem("xn_ok")
        acc1_ok = sem("acc1_ok")
        mod1_pe = sem("mod1_pe")
        mod1_ok = sem("mod1_ok")
        nt_pe = sem("nt_pe")
        nt_act = sem("nt_act")
        nt_hi = sem("nt_hi")
        nt_lo = sem("nt_lo")
        w_begin = sem("w_begin")
        w_hi = sem("w_hi")
        w_ready = sem("w_ready")
        pj_pe = sem("pj_pe")
        pj_ev = sem("pj_ev")
        ir_st = sem("ir_st")
        ix_hi = sem("ix_hi")
        ix_ready = sem("ix_ready")
        ix_pe = sem("ix_pe")
        ix_ev = sem("ix_ev")
        ix_kb = sem("ix_kb")
        sc_pe = sem("sc_pe")
        sc_relu = sem("sc_relu")
        sc_done = sem("sc_done")
        sc_mask = sem("sc_mask")
        tk_st = sem("tk_st")
        tk_done = sem("tk_done")
        fg_v = sem("fg_v")
        fg_a = sem("fg_a")
        cum_pe = sem("cum_pe")
        cum_ev = sem("cum_ev")
        cumT_pe = sem("cumT_pe")
        cumT_ok = sem("cumT_ok")
        rope_d = sem("rope_d")
        qs_hi = sem("qs_hi")
        qs_ready = sem("qs_ready")
        kd_ready = sem("kd_ready")
        bt_a = sem("bt_a")
        bt_ready = sem("bt_ready")
        md_ms = sem("md_ms")
        md_a = sem("md_a")
        md_done = sem("md_done")
        qk_pe = sem("qk_pe")
        lg_done = sem("lg_done")
        ex_done = sem("ex_done")
        tp_pe = sem("tp_pe")
        tp_ev = sem("tp_ev")
        kb_ev = sem("kb_ev")
        pv_pe = sem("pv_pe")
        rv_ok = sem("rv_ok")
        on_done = sem("on_done")
        md_pe = sem("md_pe")
        md_ev = sem("md_ev")
        ysq = sem("ysq")
        yroot = sem("yroot")
        yrstd = sem("yrstd")
        yn_ok = sem("yn_ok")
        yt_pe = sem("yt_pe")
        yt_act = sem("yt_act")
        yt_hi = sem("yt_hi")
        yt_lo = sem("yt_lo")
        op_pe = sem("op_pe")
        op_mul = sem("op_mul")
        x1_ok = sem("x1_ok")
        h2_root = sem("h2_root")
        h2_sq = sem("h2_sq")
        h2_rstd = sem("h2_rstd")
        h2_xn = sem("h2_xn")
        h2_pe = sem("h2_pe")
        h2_act = sem("h2_act")
        h2_hi = sem("h2_hi")
        h2_lo = sem("h2_lo")
        g_pe = sem("g_pe")
        u_pe = sem("u_pe")
        silu_ok = sem("silu_ok")
        mul_ok = sem("mul_ok")
        gu_hi = sem("gu_hi")
        gu_ready = sem("gu_ready")
        dn_pe = sem("dn_pe")
        dn_mul = sem("dn_mul")
        acc_ok = sem("acc_ok")
        fin_sq = sem("fin_sq")
        fin_root = sem("fin_root")
        fin_rstd = sem("fin_rstd")
        fin_ok = sem("fin_ok")

        raw_target = {}
        count = [0, 0]
        for n in range(N_FFN0):
            count[n % 2] += 32 if n < PIECES else 16
            raw_target[n] = count[n % 2]
        raw_base = list(count)

        SMALL = 16 * 7
        GROUPS = 2 * NH // 4

        ctx.enter_context(nc.allow_non_contiguous_dma(reason="short vectors onto partitions"))
        block = ctx.enter_context(nc.Block())

        @block.sync
        def _(sp):
            def load_piece(n):
                ch, j = divmod(n, PIECES)
                if n >= 2:
                    sp.wait_ge(w_ready, n - 1)
                w = IDXW if ch == 0 else GW
                dst = raw[:, n % 2, 0:2 * w].rearrange("p (a n) -> p a n", a=2)
                src = w_in[2 * j * P:(2 * j + 2) * P, :].rearrange("(a p) n -> p a n", p=P)
                w0 = IDXW - NH if ch == 0 else GW
                sp.dma_start(dst[:, :, 0:w0], src[:, :, CHUNK_COL[ch]:CHUNK_COL[ch] + w0]).then_inc(raw_in[n % 2], 16)
                if ch == 0:
                    sp.dma_start(dst[:, :, w0:w], src[:, :, COL_F:COL_F + NH]).then_inc(raw_in[n % 2], 16)

            def load_ada(k):
                if k >= 3:
                    sp.wait_ge(acc1_ok, k - 2)
                sp.dma_start(ada1[:, k % 3, :], ada_w[k * P:(k + 1) * P, 0:2 * D]).then_inc(ada_in[k % 3], 16)

            sp.dma_start(ccol[:], c.rearrange("(k p) -> p k", p=P)).then_inc(small_in, 16)
            sp.dma_start(posi[:], positions.rearrange("(t p) -> p t", p=P)).then_inc(small_in, 16)
            for t in range(2):
                sp.dma_start(xs[:, t, :], x[t * P:(t + 1) * P, :]).then_inc(x_in[t], 16)
            for k in range(3):
                load_ada(k)
            sp.dma_start(gains[:, 0, :], norm_attn_g[0].rearrange("(k p) -> p k", p=P)).then_inc(small_in, 16)
            sp.dma_start(gains[:, 1, 0:4], dsa_norm_g[0].rearrange("(k p) -> p k", p=P)).then_inc(small_in, 16)
            sp.dma_start(gains[:, 1, 4:8], fox_norm_g[0].rearrange("(k p) -> p k", p=P)).then_inc(small_in, 16)
            sp.dma_start(gains[:, 2, :], norm_ffn_g[0].rearrange("(k p) -> p k", p=P)).then_inc(small_in, 16)
            sp.dma_start(bfor[:], b_forget[0:1, :].to_broadcast([P, NH])).then_inc(small_in, 16)
            sp.wait_ge(const_ok, 1)
            sp.dma_start(acc1[0:1, :], ada_b[0:2 * D].rearrange("(a n) -> a n", a=1)).then_inc(bias1_in, 16)
            for k in range(3, KT):
                load_ada(k)
                t = k - 1
                sp.dma_start(xs[:, t, :], x[t * P:(t + 1) * P, :]).then_inc(x_in[t], 16)
            sp.dma_start(xs[:, TT - 1, :], x[(TT - 1) * P:, :]).then_inc(x_in[TT - 1], 16)
            for n in range(2 * PIECES):
                load_piece(n)
            for ch in range(1, NC):
                for t in range(TT):
                    q = TT * (ch - 1) + t
                    sp.wait_ge(pj_ev, TT * ch + t + 1)
                    sp.dma_start(qkv[ch - 1, t * P:(t + 1) * P, :], stage[:, q % 2, :]).then_inc(stage_out[q % 2], 16)
                    if t < PIECES and ch + 1 < NC:
                        load_piece(PIECES * (ch + 1) + t)
                if ch == 3:
                    sp.wait_ge(cumT_ok, 1)
                    sp.dma_start(cum_dram.rearrange("h (t p) -> (h t) p", p=P), cumT[:]).then_inc(cum_out, 16)

            def load_heads(g):
                first = 0 if g < GROUPS // 2 else 3
                cols = slice((g % 2) * 4 * DH, (g % 2 + 1) * 4 * DH)
                if g == 2:
                    sp.wait_ge(kd_ready, 4)
                    sp.wait_ge(qs_ready, 4)
                    sp.wait_ge(pv_pe, 4 * TT)
                if g == 3:
                    sp.wait_ge(kd_ready, 8)
                    sp.wait_ge(qs_ready, 8)
                    sp.wait_ge(pv_pe, 8 * TT)
                for i, dst in enumerate((Qn, Kn, Vn)):
                    src = qkv[first + i].rearrange("(t p) n -> p t n", p=P)[:, :, cols]
                    sp.dma_start(dst[:, g % 2, :, :], src).then_inc(qkv_in[g % 2], 16)

            def load_cum(hd):
                if hd >= 2:
                    sp.wait_ge(bt_ready, TT * (hd - 1))
                sp.dma_start(ckb[:, hd % 2, :], cum_dram[hd:hd + 1, :].to_broadcast([P, SEQ])).then_inc(ckb_in[hd % 2], 16)

            def load_mod(n):
                i, k = divmod(n, KT)
                if n >= 2:
                    sp.wait_ge(md_a, n - 1)
                sp.dma_start(adar[:, n % 2, :], ada_w[k * P:(k + 1) * P, (2 + i) * D:(3 + i) * D]).then_inc(mod_in[n % 2], 16)

            for i in range(2):
                sp.wait_ge(stage_out[i], 16 * (NC - 1) * TT // 2)
            sp.wait_ge(w_ready, N_PROJ)
            sp.wait_ge(pj_pe, NC * TT)
            sp.wait_ge(sc_pe, IH * (TT - FIRST_TOPK))
            sp.wait_ge(cum_out, 16)
            load_heads(0)
            load_cum(0)
            load_cum(1)
            load_heads(1)
            sp.wait_ge(md_ms, 3)
            for i, dst in enumerate((g1b[0:1, :], mod23[0:1, 0, :], mod23[0:1, 1, :], g2b[0:1, :])):
                sp.dma_start(dst, ada_b[(2 + i) * D:(3 + i) * D].rearrange("(a n) -> a n", a=1)).then_inc(mod_bias_in, 16)
            for hd in range(2 * NH):
                if hd == 4:
                    load_heads(2)
                if hd == 8:
                    load_heads(3)
                load_mod(2 * hd)
                load_mod(2 * hd + 1)
                if hd + 2 < NH:
                    load_cum(hd + 2)

            sp.wait_ge(pv_pe, UNITS)
            sp.wait_ge(md_done, 4 * KT)
            sp.wait_ge(md_pe, 2)
            for k in range(KT):
                n = N_PROJ + k
                if k >= 2:
                    sp.wait_ge(w_ready, n - 1)
                sp.dma_start(raw2[:, n % 2, :], w_out[k * P:(k + 1) * P, :]).then_inc(raw_in[n % 2], 16)
                if k < 2:
                    sp.dma_start(xr[:, k, :], x[k * P:(k + 1) * P, :]).then_inc(xr_in[k], 16)
            for j in range(2):
                sp.wait_ge(w_ready, N_FFN0 + j - 1)
                src = (w_gate, w_up)[j][:, 0:P].rearrange("(k p) n -> p k n", p=P)
                sp.dma_start(raw2[:, j, :].rearrange("p (k n) -> p k n", k=KT), src).then_inc(raw_in[j], 16)
            for t in range(2, TT):
                sp.wait_ge(h2_pe, 2 * (t - 1))
                sp.dma_start(xr[:, t % 2, :], x[t * P:(t + 1) * P, :]).then_inc(xr_in[t % 2], 16)

            def load_gu(n, j, col):
                sp.wait_ge(w_ready, n - 1)
                src = (w_gate, w_up)[j % 2][:, bass.ds(col, P)].rearrange("(k p) n -> p k n", p=P)
                sp.dma_start(raw2[:, j % 2, :].rearrange("p (k n) -> p k n", k=KT), src).then_inc(raw_in[j % 2], 16)

            def load_down(n, j, row):
                sp.wait_ge(w_ready, n - 1)
                sp.dma_start(raw2[:, j % 2, :], w_down[bass.ds(row, P), :]).then_inc(raw_in[j % 2], 16)

            for j in (2, 3):
                load_gu(N_FFN0 + j, j, P)
            with sp.Fori(1, FI) as i:
                for j in range(4):
                    load_gu(N_FFN0 + 6 * i + j, j, (2 * i + j // 2) * P)
                for j in (4, 5):
                    load_down(N_FFN0 + 6 * i + j, j, (2 * i - 2 + j - 4) * P)
            for j in range(2):
                load_down(N_FFN0 + 6 * FI + j, j, (2 * FI - 2 + j) * P)
            sp.wait_ge(w_ready, N_FFN0 + 6 * FI + 1)
            sp.dma_start(raw2[:, 0, :],
                         final_norm_g.rearrange("(a n) -> a n", a=1).to_broadcast([P, D])).then_inc(fgain_in, 16)
            for t in range(TT):
                sp.wait_ge(fin_ok, t + 1)
                sp.dma_start(out[t * P:(t + 1) * P, :], O[:, t, :]).then_inc(out_done, 16)
            sp.wait_ge(out_done, 16 * TT)

        @block.gpsimd
        def _(pool):
            pool.memset(acc1[:], 0.0).then_inc(const_ok, 1)
            pool.memset(ident[:], 0.0).then_inc(const_st, 1)
            pool.memset(ones[:], 1.0).then_inc(const_st, 1)
            pool.memset(causal[:], BIG).then_inc(const_st, 1)
            pool.memset(epsc[:], EPS).then_inc(const_st, 1)
            pool.memset(sel[:, 0:sel_off(FIRST_TOPK)], 0.0).then_inc(const_st, 1)
            pool.wait_ge(const_st, 5)
            pool.affine_select(out=ident[:], in_=ident[:], compare_op=ALU.not_equal, fill=1.0, base=0,
                               pattern=[[-1, P]], channel_multiplier=1).then_inc(const_ok, 1)
            pool.affine_select(out=tri[:], in_=ones[:], compare_op=ALU.is_ge, fill=0.0, base=0,
                               pattern=[[1, P]], channel_multiplier=-1).then_inc(const_ok, 1)
            pool.affine_select(out=causal[:], in_=causal[:], compare_op=ALU.is_gt, fill=0.0, base=0,
                               pattern=[[1, P]], channel_multiplier=-1).then_inc(const_ok, 1)
            pool.wait_ge(const_ok, 4)
            for t in range(FIRST_TOPK):
                o = sel_off(t) + t * P
                pool.tensor_copy(sel[:, o:o + P], causal[:]).then_inc(const_ok, 1)

            def split(n, hi, lo, src, inc=1):
                pool.tensor_copy(hi, src).then_inc(w_hi, inc)
                pool.wait_ge(w_hi, n + 1)
                return pool.tensor_tensor(lo, src, hi.bitcast(F32), ALU.subtract)

            for n in range(N_PROJ):
                ch = n // PIECES
                w = IDXW if ch == 0 else GW
                pool.wait_ge(raw_in[n % 2], raw_target[n])
                if ch == 1 and n % PIECES == 0:
                    pool.wait_ge(nt_pe, 2 * KT)
                if ch >= 2:
                    pool.wait_ge(pj_pe, TT * (ch - 1))
                hi, lo = wsl(n)
                split(n, hi[:, 0:2 * w], lo[:, 0:2 * w], raw[:, n % 2, 0:2 * w]).then_inc(w_ready, 1)

            pool.wait_ge(pj_pe, NC * TT)
            for dst in (g1b, g2b, mod23):
                pool.memset(dst[:], 0.0).then_inc(md_ms, 1)

            steps = {"rope": 0, "bt": 0}

            def rotary(g):
                for v in (Qn, Kn):
                    v4 = v[:, g % 2, :, :].rearrange("p t (h d) -> p t h d", d=DH)
                    x1, x2 = v4[:, :, :, 0:HALF], v4[:, :, :, HALF:ROT]
                    co = cosT[:].unsqueeze(2).to_broadcast([P, TT, 4, HALF])
                    si = sinT[:].unsqueeze(2).to_broadcast([P, TT, 4, HALF])
                    tm = [adat[:, i * 256:(i + 1) * 256].rearrange("p (t h d) -> p t h d", t=TT, h=4) for i in range(4)]
                    for dst, a, b in ((tm[0], x1, co), (tm[1], x2, si), (tm[2], x2, co), (tm[3], x1, si)):
                        pool.tensor_tensor(dst, a, b, ALU.mult).then_inc(rope_d, 1)
                    steps["rope"] += 4
                    pool.wait_ge(rope_d, steps["rope"])
                    pool.tensor_tensor(x1, tm[0], tm[1], ALU.subtract).then_inc(rope_d, 1)
                    pool.tensor_tensor(x2, tm[2], tm[3], ALU.add).then_inc(rope_d, 1)
                    steps["rope"] += 2
                    pool.wait_ge(rope_d, steps["rope"])

            def prepare(hd):
                g = hd // 4
                pool.wait_ge(qkv_in[g % 2], 48 * (g // 2 + 1))
                cols = slice((hd % 4) * DH, (hd % 4 + 1) * DH)
                q, k = Qn[:, g % 2, :, cols], Kn[:, g % 2, :, cols]
                if hd >= 1:
                    pool.wait_ge(tp_pe, group_no[("P", hd - 1, 3)] + 1)
                pool.tensor_copy(qs[:, :, 0, :].bitcast(F32R), q).then_inc(qs_hi, 1)
                pool.tensor_copy(kd[:], k.unsqueeze(2).to_broadcast([P, TT, 2, DH])).then_inc(kd_ready, 1)
                pool.wait_ge(qs_hi, hd + 1)
                pool.tensor_tensor(qs[:, :, 1, :], q, qs[:, :, 0, :], ALU.subtract).then_inc(qs_ready, 1)

            def fox_bias(u):
                hd, t = divmod(u, TT)
                n = P * (t + 1)
                if t == 0:
                    pool.wait_ge(ckb_in[hd % 2], 16 * (hd // 2 + 1))
                if u >= 2:
                    pool.wait_ge(lg_done, u - 1)
                pool.tensor_scalar(bt[:, u % 2, 0:n], ckb[:, hd % 2, 0:n], ncumq[:, hd * TT + t:hd * TT + t + 1], 1.0,
                                   ALU.add, ALU.mult).then_inc(bt_a, 1)
                pool.wait_ge(bt_a, u + 1)
                pool.tensor_tensor(bt[:, u % 2, n - P:n], bt[:, u % 2, n - P:n], causal[:], ALU.add).then_inc(bt_ready, 1)

            sums_of = [g1b[:], mod23[:, 0, :], mod23[:, 1, :], g2b[:]]

            def modulation(n):
                i, k = divmod(n, KT)
                if n == 0:
                    pool.wait_ge(mod_bias_in, 64)
                pool.wait_ge(mod_in[n % 2], 16 * (n // 2 + 1))
                if n >= 1:
                    pool.wait_ge(md_done, n)
                pool.tensor_scalar(adat[:], adar[:, n % 2, :], cact[:, k:k + 1], 1.0, ALU.mult, ALU.mult).then_inc(md_a, 1)
                pool.wait_ge(md_a, n + 1)
                pool.tensor_tensor(sums_of[i], sums_of[i], adat[:], ALU.add).then_inc(md_done, 1)

            prepare(0)
            for hd in range(2 * NH):
                for t in range(TT):
                    if hd < NH:
                        fox_bias(hd * TT + t)
                    if t == 1 and hd + 1 < 2 * NH:
                        if hd + 1 in (8, 12):
                            g = (hd + 1) // 4
                            pool.wait_ge(qkv_in[g % 2], 96)
                            if hd > 0:
                                pool.wait_ge(md_done, 2 * hd)
                            rotary(g)
                        prepare(hd + 1)
                    if t in (4, 6):
                        modulation(2 * hd + (t == 6))

            for k in range(KT):
                n = N_PROJ + k
                pool.wait_ge(raw_in[n % 2], raw_target[n])
                hi, lo = osl(k)
                split(n, hi, lo, raw2[:, n % 2, :]).then_inc(w_ready, 1)

            def split_ffn(n, j, uses, slot, inc=1):
                pool.wait_ge(raw_in[j % 2], uses)
                pool.sem_inc(w_begin, 1)
                split(n, vh[:, slot, :], vl[:, slot, :], raw2[:, j % 2, :], inc).then_inc(w_ready, inc)

            pool.wait_ge(op_pe, 2 * TT)
            for j in range(4):
                split_ffn(N_FFN0 + j, j, raw_base[j % 2] + 16 * (j // 2 + 1), j, 3 if j == 3 else 1)
            with pool.Fori(1, FI) as i:
                for j in range(6):
                    if j < 4:
                        pool.wait_ge(u_pe if j % 2 else g_pe, 4 * (i - 1) + 2 * (j // 2) + 2)
                    elif j == 4:
                        pool.wait_ge(dn_pe, 16 * i)
                    split_ffn(N_FFN0 + 6 * i + j, j, raw_base[j % 2] + 32 + 48 * (i - 1) + 16 * (j // 2 + 1), j)
            for j in range(2):
                pool.wait_ge(u_pe if j else g_pe, 4 * (FI - 1) + 2)
                split_ffn(N_FFN0 + 6 * FI + j, j, raw_base[j % 2] + 32 + 48 * (FI - 1) + 16, j)

        @block.scalar
        def _(act):
            act.wait_ge(small_in, SMALL)
            act.activation(cact[:], ccol[:], ACT.Silu).then_inc(cact_ok, 1)
            act.wait_ge(rope_st, ROPE_STEPS)
            act.activation(sinT[:].rearrange("p t j -> p (t j)"), rp[:, 2, :], ACT.Sin).then_inc(rope_sin, 1)
            act.activation(cosT[:].rearrange("p t j -> p (t j)"), rp[:, 3, :], ACT.Sin).then_inc(rope_sin, 1)
            for t in range(TT):
                act.wait_ge(x_in[t], 16)
                if t >= 1:
                    act.wait_ge(ssq_ok, t)
                act.activation(PS[:, 0:2, :].rearrange("p a b -> p (a b)"), xs[:, t, :], ACT.Square,
                               accum_out=stat[:, 0, t:t + 1]).then_inc(ssq_ok, 1)
            act.wait_ge(ssq_ok, TT)
            act.wait_ge(const_ok, 4)
            act.activation(stat[:, 1, 0:TT], stat[:, 0, 0:TT], ACT.Sqrt, bias=epsc[:], scale=1.0 / D).then_inc(root_ok, 1)
            act.wait_ge(mod1_ok, 2)
            for g in range(2 * KT):
                k = g % KT
                act.wait_ge(nt_pe, g + 1)
                if g >= 2:
                    act.wait_ge(nt_lo, g - 1)
                act.activation(hf1[:, g % 2, :], PS[:, 4 + g % 4, :], ACT.Identity, bias=shiftB[:, 0, k:k + 1],
                               scale=scaleA[:, 0, k:k + 1]).then_inc(nt_act, 1)

            def evac_tile(ch, t):
                q = TT * ch + t
                act.wait_ge(pj_pe, q + 1)
                if ch == 0:
                    if t == 0:
                        act.wait_ge(nt_lo, 2 * KT)
                    act.mul(idxn[:, t, 0:IH * DH], PS[:, q % 4, 0:IH * DH], SOFT)
                    act.copy(idxn[:, t, IH * DH:IDXW], PS[:, q % 4, IH * DH:IDXW]).then_inc(pj_ev, 1)
                    return
                n = q - TT
                if n >= 2:
                    act.wait_ge(stage_out[n % 2], 16 * (n // 2))
                act.mul(stage[:, n % 2, :], PS[:, q % 4, :], -SOFT if ch in (1, 4) else 1.0).then_inc(pj_ev, 1)

            def evac_item(m):
                for half in range(2):
                    g = 2 * m + half
                    act.wait_ge(ix_pe, g + 1)
                    cols = slice(half * BANK, (half + 1) * BANK)
                    dst = kai[:, cols] if m == 0 else qti[:, m - 1, cols]
                    act.copy(dst, PS[:, 4 + g % 4, :]).then_inc(ix_ev, 1)

            def relu_scores(t):
                n = P * (t + 1)
                for h in range(IH):
                    si = IH * (t - FIRST_TOPK) + h
                    act.wait_ge(sc_pe, si + 1)
                    b = 4 + 2 * (si % 2)
                    v = PS[:, b:b + 2, :].rearrange("p a b -> p (a b)")[:, 0:n]
                    act.activation(v, v, ACT.Relu).then_inc(sc_relu, 1)

            def forget():
                act.wait_ge(fg_v, 3)
                act.activation(fg[:, 1, :], fg[:, 1, :], ACT.Exp).then_inc(fg_a, 1)
                act.wait_ge(fg_a, 1)
                act.activation(fg[:, 1, :], fg[:, 1, :], ACT.Ln, bias=1.0).then_inc(fg_a, 1)
                act.wait_ge(cum_pe, 1)
                act.copy(cumq[:], PS[:, 4, 0:NH * TT]).then_inc(cum_ev, 1)
                act.mul(ncumq[:], PS[:, 4, 0:NH * TT], -1.0).then_inc(cum_ev, 1)
                act.wait_ge(cumT_pe, 1)
                act.copy(cumT[:], PS[0:NH * TT, 5, 0:P]).then_inc(cumT_ok, 1)

            for step in PROJ_ORDER:
                if step[0] == "tile":
                    evac_tile(step[1], step[2])
                elif step[0] == "item":
                    evac_item(step[1])
                elif step[0] == "score":
                    relu_scores(step[1])
                else:
                    forget()

            def evac_group(g):
                n = group_no[g]
                act.wait_ge(tp_pe, n + 1)
                src = PS[:, 4 + n % 2, :]
                if g[0] == "P":
                    hd, part = g[1], g[2]
                    if hd >= 2:
                        act.wait_ge(qk_pe, TT * (hd - 1))
                    dst = (QT if part < 2 else KA)[:, hd % 2, (part % 2) * BANK:(part % 2 + 1) * BANK]
                    act.copy(dst, src).then_inc(tp_ev, 1)
                else:
                    u, b = g[1], g[2]
                    w = halves(P * (u % TT + 1))[b][1]
                    if u >= 2 and b == 0:
                        act.wait_ge(pv_pe, u - 1)
                    act.copy(PT[:, u % 2, b * BANK:b * BANK + w], src[:, 0:w]).then_inc(tp_ev, 1)

            def expo(u):
                n = P * (u % TT + 1)
                act.wait_ge(lg_done, u + 1)
                act.activation(LP[:, u % 3, 0:n], LP[:, u % 3, 0:n], ACT.Exp, bias=nmin[:, u:u + 1], scale=-1.0,
                               accum_out=sums[:, u:u + 1]).then_inc(ex_done, 1)

            def squares(kind, first):
                for t in range(TT):
                    if first + t >= 1:
                        act.wait_ge(ysq, first + t)
                    act.activation(PS[:, 5, :], O[:, t, kind * GW:(kind + 1) * GW], ACT.Square,
                                   accum_out=stat[:, 2, kind * TT + t:kind * TT + t + 1]).then_inc(ysq, 1)

            for part in range(4):
                evac_group(("P", 0, part))
            for s in range(UNITS + 2):
                hd, t = divmod(s, TT)
                if s < UNITS and 1 <= t <= 4 and hd + 1 < 2 * NH:
                    evac_group(("P", hd + 1, t - 1))
                if s >= 2:
                    for b in range(len(halves(P * ((s - 2) % TT + 1)))):
                        evac_group(("T", s - 2, b))
                if s < UNITS:
                    expo(s)

            act.wait_ge(md_pe, 1)
            act.copy(g1b[:], PS[:, 0:2, :].rearrange("p a b -> p (a b)")).then_inc(md_ev, 1)
            act.copy(g2b[:], PS[:, 2:4, :].rearrange("p a b -> p (a b)")).then_inc(md_ev, 1)
            act.wait_ge(on_done, 2 * NH)
            squares(0, 0)
            squares(1, TT)
            act.wait_ge(ysq, 2 * TT)
            act.activation(stat[:, 3, :], stat[:, 2, :], ACT.Sqrt, bias=epsc[:], scale=1.0 / GW).then_inc(yroot, 1)
            for g in range(2 * KT):
                act.wait_ge(yt_pe, g + 1)
                if g >= 2:
                    act.wait_ge(yt_lo, g - 1)
                act.activation(hf2[:, g % 2, :], PS[:, 4 + g % 4, :], ACT.Identity,
                               scale=gains[:, 1, g % KT:g % KT + 1]).then_inc(yt_act, 1)

            def root2(t):
                act.wait_ge(x1_ok, 2 * t + 2)
                act.activation(PS[:, 4:6, :].rearrange("p a b -> p (a b)"), O[:, t, :], ACT.Square,
                               accum_out=stat[:, 0, t:t + 1]).then_inc(h2_sq, 1)
                act.wait_ge(h2_sq, t + 1)
                act.activation(stat[:, 1, t:t + 1], stat[:, 0, t:t + 1], ACT.Sqrt, bias=epsc[:],
                               scale=1.0 / D).then_inc(h2_root, 1)

            def scale2(t):
                for kh in range(2):
                    g = 2 * t + kh
                    act.wait_ge(h2_pe, g + 1)
                    if g >= 2:
                        act.wait_ge(h2_lo, g - 1)
                    for i in range(4):
                        k = 4 * kh + i
                        last = act.activation(hf2[:, g % 2, i * P:(i + 1) * P], PS[:, 6 + g % 2, i * P:(i + 1) * P],
                                              ACT.Identity, bias=shiftB[:, 1, k:k + 1], scale=scaleA[:, 1, k:k + 1])
                    last.then_inc(h2_act, 1)

            act.wait_ge(yt_lo, 2 * KT)
            for s in range(TT + 2):
                if s < TT:
                    root2(s)
                if s >= 2:
                    scale2(s - 2)

            def gated(i, par, first=False):
                for a in range(2):
                    for hf in range(2):
                        idx = 4 * i + 2 * a + hf
                        act.wait_ge(g_pe, idx + 1)
                        if not (first and a == 0):
                            act.wait_ge(mul_ok, idx - 1)
                        act.activation(sil[:, hf, :], PS[:, hf, :], ACT.Silu).then_inc(silu_ok, 1)
                    for hf in range(2):
                        idx = 4 * i + 2 * a + hf
                        act.wait_ge(mul_ok, idx + 1)
                        act.copy(guh[:, par, a, hf * BANK:(hf + 1) * BANK], gf[:, hf, :]).then_inc(gu_hi, 1)

            gated(0, 0, True)
            with act.Fori(1, FI, 2) as i0:
                for odd in range(2):
                    i = i0 + odd
                    act.wait_ge(dn_pe, 16 * i)
                    gated(i, 1 - odd)
            for t in range(TT):
                act.wait_ge(acc_ok, 16 * FI + 2 * t + 2)
                act.activation(PS[:, 0:2, :].rearrange("p a b -> p (a b)"), O[:, t, :], ACT.Square,
                               accum_out=stat[:, 0, t:t + 1]).then_inc(fin_sq, 1)
                act.wait_ge(fin_sq, t + 1)
                act.activation(stat[:, 1, t:t + 1], stat[:, 0, t:t + 1], ACT.Sqrt, bias=epsc[:],
                               scale=1.0 / D).then_inc(fin_root, 1)

        @block.vector
        def _(dve):
            ang, turns, red, red2 = (rp[:, i, :] for i in range(4))
            n_rope = 0

            def rope_step(ins):
                nonlocal n_rope
                n_rope += 1
                ins.then_inc(rope_st, 1)
                dve.wait_ge(rope_st, n_rope)

            dve.wait_ge(small_in, SMALL)
            rope_step(dve.tensor_copy(posf[:], posi[:]))
            for j in range(HALF):
                rope_step(dve.tensor_scalar(ang.rearrange("p (t j) -> p t j", t=TT)[:, :, j], posf[:],
                                            float(INV_FREQ[j]), None, ALU.mult))
            rope_step(dve.tensor_scalar(turns, ang, 1.0 / (2 * np.pi), RMAGIC, ALU.mult, ALU.add))
            rope_step(dve.tensor_scalar(turns, turns, -RMAGIC, None, ALU.add))
            rope_step(dve.scalar_tensor_tensor(out=red, in0=turns, scalar=-TWO_PI_A, in1=ang, op0=ALU.mult, op1=ALU.add))
            rope_step(dve.scalar_tensor_tensor(out=red, in0=turns, scalar=-TWO_PI_B, in1=red, op0=ALU.mult, op1=ALU.add))
            rope_step(dve.scalar_tensor_tensor(out=red, in0=turns, scalar=-TWO_PI_C, in1=red, op0=ALU.mult, op1=ALU.add))
            rope_step(dve.tensor_scalar(red, red, PI_IN, -PI_IN, ALU.min, ALU.max))
            rope_step(dve.tensor_scalar(red2, red, np.pi / 2, None, ALU.add))
            rope_step(dve.tensor_scalar(turns, red2, PI_IN, -2 * np.pi, ALU.is_gt, ALU.mult))
            rope_step(dve.tensor_tensor(red2, red2, turns, ALU.add))
            rope_step(dve.tensor_scalar(red2, red2, PI_IN, -PI_IN, ALU.min, ALU.max))
            assert n_rope == ROPE_STEPS

            dve.wait_ge(cact_ok, 1)
            dve.wait_ge(bias1_in, 16)
            for k in range(KT):
                dve.wait_ge(ada_in[k % 3], 16 * (k // 3 + 1))
                if k >= 1:
                    dve.wait_ge(acc1_ok, k)
                dve.scalar_tensor_tensor(out=acc1[:], in0=ada1[:, k % 3, :], scalar=cact[:, k:k + 1], in1=acc1[:],
                                         op0=ALU.mult, op1=ALU.add).then_inc(acc1_ok, 1)
            dve.wait_ge(root_ok, 1)
            dve.reciprocal(rstd[:, 0, 0:TT], stat[:, 1, 0:TT]).then_inc(rstd_ok, 1)
            dve.wait_ge(rstd_ok, 1)
            for t in range(TT):
                dve.tensor_scalar(xs[:, t, :], xs[:, t, :], rstd[:, 0, t:t + 1], None, ALU.mult).then_inc(xn_ok, 1)
            dve.wait_ge(mod1_pe, 1)
            dve.tensor_copy(shiftB[:, 0, :], PS[:, 2, 0:KT]).then_inc(mod1_ok, 1)
            dve.scalar_tensor_tensor(out=scaleA[:, 0, :], in0=PS[:, 2, KT:2 * KT], scalar=1.0, in1=gains[:, 0, :],
                                     op0=ALU.add, op1=ALU.mult).then_inc(mod1_ok, 1)
            for g in range(2 * KT):
                k, half = g % KT, g // KT
                cols = slice(half * BANK, (half + 1) * BANK)
                dve.wait_ge(nt_act, g + 1)
                dve.tensor_copy(hh[:, k, cols], hf1[:, g % 2, :]).then_inc(nt_hi, 1)
                dve.wait_ge(nt_hi, g + 1)
                dve.tensor_tensor(hl[:, k, cols], hf1[:, g % 2, :], hh[:, k, cols].bitcast(F32), ALU.subtract).then_inc(nt_lo, 1)

            dve.wait_ge(pj_ev, TT)
            dve.wait_ge(rope_sin, 2)
            v4 = idxn[:, :, 0:(IH + 1) * DH].rearrange("p t (h d) -> p t h d", d=DH)
            x1, x2 = v4[:, :, :, 0:HALF], v4[:, :, :, HALF:ROT]
            co = cosT[:].unsqueeze(2).to_broadcast([P, TT, IH + 1, HALF])
            si = sinT[:].unsqueeze(2).to_broadcast([P, TT, IH + 1, HALF])
            tm = [rot[:, i, :].rearrange("p (t h d) -> p t h d", t=TT, h=IH + 1) for i in range(4)]
            for dst, a, b in ((tm[0], x1, co), (tm[1], x2, si), (tm[2], x2, co), (tm[3], x1, si)):
                dve.tensor_tensor(dst, a, b, ALU.mult).then_inc(ir_st, 1)
            dve.wait_ge(ir_st, 4)
            dve.tensor_tensor(x1, tm[0], tm[1], ALU.subtract).then_inc(ir_st, 1)
            dve.tensor_tensor(x2, tm[2], tm[3], ALU.add).then_inc(ir_st, 1)
            dve.tensor_scalar(iws[:], idxn[:, :, (IH + 1) * DH:(IH + 1) * DH + IH], IH ** -0.5, None,
                              ALU.mult).then_inc(ir_st, 1)
            dve.wait_ge(ir_st, 7)

            def index_item(m):
                if m >= 2:
                    dve.wait_ge(ix_pe, 2 * (m - 1))
                if m == 0:
                    k = idxn[:, :, IH * DH:(IH + 1) * DH]
                    dve.tensor_copy(ixs[:, 0], k.unsqueeze(2).to_broadcast([P, TT, 2, DH])).then_inc(ix_ready, 1)
                    return
                q = idxn[:, :, (m - 1) * DH:m * DH]
                dve.tensor_copy(ixs[:, m % 2, :, 0, :].bitcast(F32R), q).then_inc(ix_hi, 1)
                dve.wait_ge(ix_hi, m)
                dve.tensor_tensor(ixs[:, m % 2, :, 1, :], q, ixs[:, m % 2, :, 0, :], ALU.subtract).then_inc(ix_ready, 1)

            index_item(0)
            index_item(1)
            for half in range(2):
                cols = slice(half * BANK, (half + 1) * BANK)
                dve.wait_ge(ix_ev, half + 1)
                dve.tensor_tensor(kbi[:, cols], PS[:, 4 + half, :], kai[:, cols].bitcast(F32), ALU.subtract).then_inc(ix_kb, 1)
            for m in range(2, IH + 1):
                index_item(m)

            fht = [fg[:, i, :].rearrange("p (h t) -> p h t", h=NH) for i in range(4)]
            dve.tensor_tensor(fht[0], idxn[:, :, IDXW - NH:IDXW].rearrange("p t h -> p h t"),
                              bfor[:].unsqueeze(2).to_broadcast([P, NH, TT]), ALU.add).then_inc(fg_v, 1)
            dve.wait_ge(fg_v, 1)
            dve.tensor_scalar(fg[:, 2, :], fg[:, 0, :], 0.0, None, ALU.min).then_inc(fg_v, 1)
            dve.scalar_tensor_tensor(out=fg[:, 1, :], in0=fg[:, 0, :], scalar=-1.0, in1=fg[:, 0, :],
                                     op0=ALU.mult, op1=ALU.min).then_inc(fg_v, 1)

            n_sc = 0

            def score(t):
                nonlocal n_sc
                n = P * (t + 1)
                o = sel_off(t)
                for h in range(IH):
                    dve.wait_ge(sc_relu, n_sc + 1)
                    b = 4 + 2 * (n_sc % 2)
                    v = PS[:, b:b + 2, :].rearrange("p a b -> p (a b)")[:, 0:n]
                    w = iws[:, t, h:h + 1]
                    if h == 0:
                        dve.tensor_scalar(sel[:, o:o + n], v, w, None, ALU.mult).then_inc(sc_done, 1)
                    else:
                        dve.wait_ge(sc_done, n_sc)
                        dve.scalar_tensor_tensor(out=sel[:, o:o + n], in0=v, scalar=w, in1=sel[:, o:o + n],
                                                 op0=ALU.mult, op1=ALU.add).then_inc(sc_done, 1)
                    n_sc += 1
                dve.wait_ge(sc_done, n_sc)
                dve.tensor_tensor(sel[:, o + n - P:o + n], sel[:, o + n - P:o + n], causal[:],
                                  ALU.subtract).then_inc(sc_mask, 1)

            ROUNDS = TOPK // 8
            all_rounds = [(t, r) for t in range(FIRST_TOPK, TT) for r in range(ROUNDS)]
            n_tk = 0
            n_round = 0

            def rounds(count):
                nonlocal n_tk, n_round
                for t, r in all_rounds[n_round:n_round + count]:
                    v = sel[:, sel_off(t):sel_off(t + 1)]
                    if n_tk:
                        dve.wait_ge(tk_st, n_tk)
                    if r == 0:
                        dve.wait_ge(sc_mask, t - FIRST_TOPK + 1)
                    dve.max(m8[:, r % 2, :], v).then_inc(tk_st, 1)
                    dve.wait_ge(tk_st, n_tk + 1)
                    dve.match_replace(v, m8[:, r % 2, :], v, TAKEN).then_inc(tk_st, 1)
                    n_tk += 2
                    if r == ROUNDS - 1:
                        dve.wait_ge(tk_st, n_tk)
                        dve.tensor_scalar(v, v, TAKEN / 1.5, BIG, ALU.is_ge, ALU.mult).then_inc(tk_done, 1)
                n_round += count

            for t in range(FIRST_TOPK, TT):
                score(t)
                if t < TT - 1:
                    rounds(7)
            dve.wait_ge(fg_a, 2)
            dve.tensor_tensor(fg[:, 3, :], fg[:, 2, :], fg[:, 1, :], ALU.subtract).then_inc(fg_v, 1)
            dve.memset(pre[:, :, 0], 0.0).then_inc(fg_v, 1)
            for t in range(1, TT):
                dve.wait_ge(fg_v, 4 + t)
                dve.tensor_tensor(pre[:, :, t], pre[:, :, t - 1], fht[3][:, :, t - 1], ALU.add).then_inc(fg_v, 1)
            rounds(EARLY_ROUNDS - n_round)

            def biased(u):
                hd, t = divmod(u, TT)
                n = P * (t + 1)
                if u >= 3:
                    last = len(halves(P * ((u - 3) % TT + 1))) - 1
                    dve.wait_ge(tp_pe, group_no[("T", u - 3, last)] + 1)
                if hd < NH:
                    dve.wait_ge(bt_ready, u + 1)
                    bias = bt[:, u % 2, 0:n]
                else:
                    if t >= FIRST_TOPK:
                        dve.wait_ge(tk_done, t - FIRST_TOPK + 1)
                    bias = sel[:, sel_off(t):sel_off(t + 1)]
                dve.wait_ge(qk_pe, u + 1)
                b = 2 * (u % 2)
                v = PS[:, b:b + 2, :].rearrange("p a b -> p (a b)")[:, 0:n]
                dve.tensor_tensor_reduce(out=LP[:, u % 3, 0:n], in0=v, in1=bias, scale=1.0, scalar=3e38,
                                         op0=ALU.add, op1=ALU.min, accum_out=nmin[:, u:u + 1]).then_inc(lg_done, 1)

            def key_lo(hd, part):
                n = group_no[("P", hd, part)]
                cols = slice((part % 2) * BANK, (part % 2 + 1) * BANK)
                dve.wait_ge(tp_ev, n + 1)
                dve.tensor_tensor(KB[:, hd % 2, cols], PS[:, 4 + n % 2, :], KA[:, hd % 2, cols].bitcast(F32),
                                  ALU.subtract).then_inc(kb_ev, 1)

            def normalise(hd):
                col = GW + hd * DH if hd < NH else (hd - NH) * DH
                units = slice(hd * TT, (hd + 1) * TT)
                dve.wait_ge(pv_pe, (hd + 1) * TT)
                dve.reciprocal(rinv[:, units], sums[:, units]).then_inc(rv_ok, 1)
                dve.wait_ge(rv_ok, hd + 1)
                dve.tensor_tensor(O[:, :, col:col + DH], PS[:, 6 + hd % 2, :].rearrange("p (t d) -> p t d", t=TT),
                                  rinv[:, units].unsqueeze(2).to_broadcast([P, TT, DH]), ALU.mult).then_inc(on_done, 1)

            key_lo(0, 2)
            key_lo(0, 3)
            for s in range(UNITS):
                hd, t = divmod(s, TT)
                if t in (3, 4) and hd + 1 < 2 * NH:
                    key_lo(hd + 1, t - 1)
                biased(s)
                if t == 3 and hd >= 1:
                    normalise(hd - 1)
                if 2 <= s and n_round < len(all_rounds):
                    rounds(1)
            normalise(2 * NH - 1)

            dve.wait_ge(md_pe, 2)
            dve.tensor_copy(shiftB[:, 1, :], PS[:, 4, 0:KT]).then_inc(md_ev, 1)
            dve.scalar_tensor_tensor(out=scaleA[:, 1, :], in0=PS[:, 4, KT:2 * KT], scalar=1.0, in1=gains[:, 2, :],
                                     op0=ALU.add, op1=ALU.mult).then_inc(md_ev, 1)
            dve.wait_ge(yroot, 1)
            dve.reciprocal(rstd[:, 1, :], stat[:, 3, :]).then_inc(yrstd, 1)
            dve.wait_ge(yrstd, 1)
            for t in range(TT):
                for kind in range(2):
                    v = O[:, t, kind * GW:(kind + 1) * GW]
                    r = kind * TT + t
                    dve.tensor_scalar(v, v, rstd[:, 1, r:r + 1], None, ALU.mult).then_inc(yn_ok, 1)
            for g in range(2 * KT):
                k, half = g % KT, g // KT
                cols = slice(half * BANK, (half + 1) * BANK)
                dve.wait_ge(yt_act, g + 1)
                dve.tensor_copy(yh[:, k, cols], hf2[:, g % 2, :]).then_inc(yt_hi, 1)
                dve.wait_ge(yt_hi, g + 1)
                dve.tensor_tensor(yl[:, k, cols], hf2[:, g % 2, :], yh[:, k, cols].bitcast(F32), ALU.subtract).then_inc(yt_lo, 1)

            dve.wait_ge(md_ev, 4)
            for s in range(TT + 2):
                if s < TT:
                    t = s
                    dve.wait_ge(xr_in[t % 2], 16 * (t // 2 + 1))
                    for nh in range(2):
                        q = 2 * t + nh
                        cols = slice(nh * BANK, (nh + 1) * BANK)
                        dve.wait_ge(op_pe, q + 1)
                        dve.tensor_tensor(tmp[:, q % 2, :], PS[:, q % 4, :], g1b[:, cols], ALU.mult).then_inc(op_mul, 1)
                        dve.wait_ge(op_mul, q + 1)
                        dve.tensor_tensor(O[:, t, cols], tmp[:, q % 2, :], xr[:, t % 2, cols], ALU.add).then_inc(x1_ok, 1)
                    dve.wait_ge(h2_root, t + 1)
                    dve.reciprocal(rstd[:, 2, t:t + 1], stat[:, 1, t:t + 1]).then_inc(h2_rstd, 1)
                    dve.wait_ge(h2_rstd, t + 1)
                    dve.tensor_scalar(xr[:, t % 2, :], O[:, t, :], rstd[:, 2, t:t + 1], None, ALU.mult).then_inc(h2_xn, 1)
                if s >= 2:
                    t = s - 2
                    for kh in range(2):
                        g = 2 * t + kh
                        dst = (slice(None), slice(4 * kh, 4 * kh + 4), slice(t * P, (t + 1) * P))
                        src = hf2[:, g % 2, :].rearrange("p (k n) -> p k n", k=4)
                        dve.wait_ge(h2_act, g + 1)
                        dve.tensor_copy(yh[dst], src).then_inc(h2_hi, 1)
                        dve.wait_ge(h2_hi, g + 1)
                        dve.tensor_tensor(yl[dst], src, yh[dst].bitcast(F32), ALU.subtract).then_inc(h2_lo, 1)

            def gated(i, par, first=False):
                for a in range(2):
                    for hf in range(2):
                        idx = 4 * i + 2 * a + hf
                        dve.wait_ge(silu_ok, idx + 1)
                        dve.wait_ge(u_pe, idx + 1)
                        if not (first and a == 0):
                            dve.wait_ge(gu_ready, idx - 1)
                        dve.tensor_tensor(gf[:, hf, :], PS[:, 2 + hf, :], sil[:, hf, :], ALU.mult).then_inc(mul_ok, 1)
                    for hf in range(2):
                        idx = 4 * i + 2 * a + hf
                        cols = slice(hf * BANK, (hf + 1) * BANK)
                        dve.wait_ge(gu_hi, idx + 1)
                        dve.tensor_tensor(gul[:, par, a, cols], gf[:, hf, :], guh[:, par, a, cols].bitcast(F32),
                                          ALU.subtract).then_inc(gu_ready, 1)

            def gather(i):
                for r in range(16):
                    q = 16 * i + r
                    t, nh = divmod(r, 2)
                    cols = slice(nh * BANK, (nh + 1) * BANK)
                    dve.wait_ge(dn_pe, 16 + q + 1)
                    dve.tensor_tensor(tmp[:, r % 2, :], PS[:, 4 + r % 4, :], g2b[:, cols], ALU.mult).then_inc(dn_mul, 1)
                    dve.wait_ge(dn_mul, q + 1)
                    dve.tensor_tensor(O[:, t, cols], tmp[:, r % 2, :], O[:, t, cols], ALU.add).then_inc(acc_ok, 1)

            dve.sem_inc(acc_ok, 16)
            gated(0, 0, True)
            with dve.Fori(1, FI, 2) as i0:
                for odd in range(2):
                    gated(i0 + odd, 1 - odd)
                    gather(i0 + odd - 1)
            gather(FI - 1)
            dve.wait_ge(fgain_in, 16)
            for t in range(TT):
                dve.wait_ge(fin_root, t + 1)
                dve.reciprocal(rstd[:, 3, t:t + 1], stat[:, 1, t:t + 1]).then_inc(fin_rstd, 1)
                dve.wait_ge(fin_rstd, t + 1)
                dve.scalar_tensor_tensor(out=O[:, t, :], in0=O[:, t, :], scalar=rstd[:, 3, t:t + 1],
                                         in1=raw2[:, 0, :], op0=ALU.mult, op1=ALU.mult).then_inc(fin_ok, 1)

        @block.tensor
        def _(pe):
            def three(dst, left, right, first, last):
                pe.matmul(dst, left[0], right[0], start=first, stop=False)
                pe.matmul(dst, left[0], right[1], start=False, stop=False)
                return pe.matmul(dst, left[1], right[0], start=False, stop=last)

            pe.wait_ge(const_ok, 4)
            pe.wait_ge(acc1_ok, KT)
            for j in range(2 * KT):
                last = pe.matmul(PS[:, 2, j:j + 1], acc1[:, j * P:(j + 1) * P], ones[:, 0:1], start=True, stop=True)
            last.then_inc(mod1_pe, 1)
            for g in range(2 * KT):
                k, half = g % KT, g // KT
                pe.wait_ge(xn_ok, 4 * (half + 1))
                if g >= 4:
                    pe.wait_ge(nt_act, g - 3)
                for i in range(4):
                    last = pe.transpose(PS[:, 4 + g % 4, i * P:(i + 1) * P], xs[:, 4 * half + i, k * P:(k + 1) * P], ident[:])
                last.then_inc(nt_pe, 1)

            def tile(ch, t):
                q = TT * ch + t
                w = IDXW if ch == 0 else GW
                if ch == 0:
                    pe.wait_ge(nt_hi, KT * (t // 4 + 1))
                    pe.wait_ge(nt_lo, KT * (t // 4 + 1))
                if q >= 4:
                    pe.wait_ge(pj_ev, q - 3)
                for k in range(KT):
                    n = PIECES * ch + k // 2
                    if t == 0 and k % 2 == 0:
                        pe.wait_ge(w_ready, n + 1)
                    cols = slice((k % 2) * w, (k % 2 + 1) * w)
                    hi, lo = wsl(n)
                    rows = slice(t * P, (t + 1) * P)
                    last = three(PS[:, q % 4, 0:w], (hh[:, k, rows], hl[:, k, rows]), (hi[:, cols], lo[:, cols]),
                                 k == 0, k == KT - 1)
                last.then_inc(pj_pe, 1)

            def item(m):
                for half in range(2):
                    g = 2 * m + half
                    pe.wait_ge(ix_ready, m + 1)
                    if g >= 4:
                        pe.wait_ge(ix_ev, g - 3)
                        pe.wait_ge(ix_kb, 2)
                    for i in range(4):
                        src = ixs[:, m % 2, 4 * half + i, :, :].rearrange("p a d -> p (a d)")
                        last = pe.transpose(PS[:, 4 + g % 4, i * P:(i + 1) * P], src, ident[:])
                    last.then_inc(ix_pe, 1)

            def index_scores(t):
                n = P * (t + 1)
                for h in range(IH):
                    si = IH * (t - FIRST_TOPK) + h
                    if si < 2:
                        pe.wait_ge(ix_ev, 2 * (IH + 1))
                        pe.wait_ge(ix_kb, 2)
                    else:
                        pe.wait_ge(sc_done, si - 1)
                    q = qti[:, h, t * P:(t + 1) * P]
                    for b, w in halves(n):
                        dst = PS[:, 4 + 2 * (si % 2) + b // BANK, 0:w]
                        pe.matmul(dst, q, kai[:, b:b + w], start=True, stop=False)
                        last = pe.matmul(dst, q, kbi[:, b:b + w], start=False, stop=True)
                    last.then_inc(sc_pe, 1)

            def cumulative():
                pe.wait_ge(sc_done, IH * (TT - FIRST_TOPK))
                pe.wait_ge(fg_v, 4 + TT)
                pe.matmul(PS[:, 4, 0:NH * TT], tri[:], fg[:, 3, :], start=True, stop=False)
                pe.matmul(PS[:, 4, 0:NH * TT], ones[:], pre[:].rearrange("p h t -> p (h t)"), start=False,
                          stop=True).then_inc(cum_pe, 1)
                pe.wait_ge(cum_ev, 1)
                pe.transpose(PS[0:NH * TT, 5, 0:P], cumq[:], ident[:]).then_inc(cumT_pe, 1)

            for step in PROJ_ORDER:
                if step[0] == "tile":
                    tile(step[1], step[2])
                elif step[0] == "item":
                    item(step[1])
                elif step[0] == "score":
                    index_scores(step[1])
                else:
                    cumulative()

            def turn(g):
                n = group_no[g]
                if n >= 2:
                    pe.wait_ge(tp_ev, n - 1)
                    if n - 2 in key_groups:
                        pe.wait_ge(kb_ev, key_groups.index(n - 2) + 1)
                dst = PS[:, 4 + n % 2, :]
                if g[0] == "P":
                    hd, part = g[1], g[2]
                    pe.wait_ge(qs_ready if part < 2 else kd_ready, hd + 1)
                    srcs = [(qs if part < 2 else kd)[:, 4 * (part % 2) + i, :, :].rearrange("p a d -> p (a d)") for i in range(4)]
                else:
                    u, b = g[1], g[2]
                    pe.wait_ge(ex_done, u + 1)
                    first, w = halves(P * (u % TT + 1))[b]
                    srcs = [LP[:, u % 3, first + i * P:first + (i + 1) * P] for i in range(w // P)]
                for i, src in enumerate(srcs):
                    last = pe.transpose(dst[:, i * P:(i + 1) * P], src, ident[:])
                last.then_inc(tp_pe, 1)

            def logits(u):
                hd, t = divmod(u, TT)
                if t == 0:
                    pe.wait_ge(tp_ev, group_no[("P", hd, 3)] + 1)
                    pe.wait_ge(kb_ev, 2 * (hd + 1))
                if u >= 2:
                    pe.wait_ge(lg_done, u - 1)
                q = QT[:, hd % 2, t * P:(t + 1) * P]
                for b, w in halves(P * (t + 1)):
                    dst = PS[:, 2 * (u % 2) + b // BANK, 0:w]
                    pe.matmul(dst, q, KA[:, hd % 2, b:b + w], start=True, stop=False)
                    last = pe.matmul(dst, q, KB[:, hd % 2, b:b + w], start=False, stop=True)
                last.then_inc(qk_pe, 1)

            def values(u):
                hd, t = divmod(u, TT)
                pe.wait_ge(tp_ev, group_no[("T", u, len(halves(P * (t + 1))) - 1)] + 1)
                if t == 0:
                    pe.wait_ge(qkv_in[(hd // 4) % 2], 48 * (hd // 8 + 1))
                    if hd >= 2:
                        pe.wait_ge(on_done, hd - 1)
                cols = slice((hd % 4) * DH, (hd % 4 + 1) * DH)
                for j in range(t + 1):
                    last = pe.matmul(PS[:, 6 + hd % 2, t * DH:(t + 1) * DH], PT[:, u % 2, j * P:(j + 1) * P],
                                     Vn[:, (hd // 4) % 2, j, cols], start=j == 0, stop=j == t)
                last.then_inc(pv_pe, 1)

            pe.wait_ge(pj_ev, NC * TT)
            pe.wait_ge(cum_ev, 2)
            pe.wait_ge(cumT_ok, 1)
            for part in range(4):
                turn(("P", 0, part))
            for s in range(UNITS + 3):
                hd, t = divmod(s, TT)
                if s < UNITS:
                    logits(s)
                if s < UNITS and 1 <= t <= 4 and hd + 1 < 2 * NH:
                    turn(("P", hd + 1, t - 1))
                if 2 <= s < UNITS + 2:
                    for b in range(len(halves(P * ((s - 2) % TT + 1)))):
                        turn(("T", s - 2, b))
                if s >= 3:
                    values(s - 3)

            pe.wait_ge(md_done, 4 * KT)
            pe.wait_ge(lg_done, UNITS)
            for i, src in enumerate((g1b, g2b)):
                for nh in range(2):
                    last = pe.matmul(PS[:, 2 * i + nh, :], ones[:], src[:, nh * BANK:(nh + 1) * BANK], start=True, stop=True)
            last.then_inc(md_pe, 1)
            pe.wait_ge(tp_ev, len(plan))
            for j in range(2 * KT):
                last = pe.matmul(PS[:, 4, j:j + 1], mod23[:, j // KT, (j % KT) * P:(j % KT + 1) * P], ones[:, 0:1],
                                 start=True, stop=True)
            last.then_inc(md_pe, 1)

            pe.wait_ge(md_ev, 4)
            pe.wait_ge(on_done, 2 * NH)
            for g in range(2 * KT):
                k, half = g % KT, g // KT
                pe.wait_ge(yn_ok, 8 * (half + 1))
                if g >= 4:
                    pe.wait_ge(yt_act, g - 3)
                for i in range(4):
                    last = pe.transpose(PS[:, 4 + g % 4, i * P:(i + 1) * P], O[:, 4 * half + i, k * P:(k + 1) * P], ident[:])
                last.then_inc(yt_pe, 1)

            for s in range(TT + 2):
                if s < TT:
                    t = s
                    rows = slice(t * P, (t + 1) * P)
                    pe.wait_ge(yt_hi, KT * (t // 4 + 1))
                    pe.wait_ge(yt_lo, KT * (t // 4 + 1))
                    for nh in range(2):
                        q = 2 * t + nh
                        cols = slice(nh * BANK, (nh + 1) * BANK)
                        if q >= 4:
                            pe.wait_ge(x1_ok, q - 3)
                        for k in range(KT):
                            if q == 0:
                                pe.wait_ge(w_ready, N_PROJ + k + 1)
                            hi, lo = osl(k)
                            last = three(PS[:, q % 4, :], (yh[:, k, rows], yl[:, k, rows]), (hi[:, cols], lo[:, cols]),
                                         k == 0, k == KT - 1)
                        last.then_inc(op_pe, 1)
                if s >= 2:
                    t = s - 2
                    pe.wait_ge(h2_xn, t + 1)
                    if t == 0:
                        pe.wait_ge(yt_act, 2 * KT)
                    for kh in range(2):
                        g = 2 * t + kh
                        if g >= 2:
                            pe.wait_ge(h2_act, g - 1)
                        for i in range(4):
                            k = 4 * kh + i
                            last = pe.transpose(PS[:, 6 + g % 2, i * P:(i + 1) * P], xr[:, t % 2, k * P:(k + 1) * P], ident[:])
                        last.then_inc(h2_pe, 1)

            def gate_up(i, first=False):
                for a in range(2):
                    for j, done, freed in ((0, g_pe, silu_ok), (1, u_pe, mul_ok)):
                        slot = 2 * a + j
                        pe.wait_ge(w_ready, N_FFN0 + 6 * i + slot + 1)
                        for hf in range(2):
                            idx = 4 * i + 2 * a + hf
                            cols = slice(hf * BANK, (hf + 1) * BANK)
                            if first and a == 0 and j == 0:
                                pe.wait_ge(h2_hi, TT * (hf + 1))
                                pe.wait_ge(h2_lo, TT * (hf + 1))
                            if not (first and a == 0):
                                pe.wait_ge(freed, idx - 1)
                            for k in range(KT):
                                w = slice(k * P, (k + 1) * P)
                                last = three(PS[:, 2 * j + hf, :], (vh[:, slot, w], vl[:, slot, w]),
                                             (yh[:, k, cols], yl[:, k, cols]), k == 0, k == KT - 1)
                            last.then_inc(done, 1)

            def down(i, par, slot, n_ready):
                pe.wait_ge(gu_ready, 4 * i + 4)
                pe.wait_ge(w_ready, n_ready)
                for r in range(16):
                    q = 16 * i + r
                    t, nh = divmod(r, 2)
                    rows = slice(t * P, (t + 1) * P)
                    cols = slice(nh * BANK, (nh + 1) * BANK)
                    pe.wait_ge(acc_ok, 16 + q - 3)
                    for a in range(2):
                        last = three(PS[:, 4 + r % 4, :], (guh[:, par, a, rows], gul[:, par, a, rows]),
                                     (vh[:, slot + a, cols], vl[:, slot + a, cols]), a == 0, a == 1)
                    last.then_inc(dn_pe, 1)

            pe.sem_inc(dn_pe, 16)
            gate_up(0, True)
            pe.wait_ge(h2_act, 2 * TT)
            with pe.Fori(1, FI, 2) as i0:
                for odd in range(2):
                    i = i0 + odd
                    gate_up(i)
                    down(i - 1, odd, 4, N_FFN0 + 6 * i + 6)
            down(FI - 1, (FI - 1) % 2, 0, N_FFN0 + 6 * FI + 2)


_INS = ['x', 'c', 'positions', 'ada_w', 'ada_b', 'norm_attn_g', 'w_in', 'b_forget', 'dsa_norm_g', 'fox_norm_g', 'w_out',
        'norm_ffn_g', 'w_gate', 'w_up', 'w_down', 'final_norm_g']


def kernel(**inputs):
    import numpy as _np
    import concourse.bacc as _bacc
    from concourse import mybir as _mybir
    from concourse.bass_utils import run_bass_kernel_spmd as _run

    nc = _bacc.Bacc("TRN2", target_bir_lowering=False, num_devices=1)
    arrays, args = {}, []
    for name in _INS:
        a = _np.ascontiguousarray(inputs[name])
        arrays[f"in_{name}_dram"] = a
        args.append(nc.dram_tensor(f"in_{name}_dram", a.shape, _mybir.dt.from_np(a.dtype), kind="ExternalInput").ap())
    args.append(nc.dram_tensor("out_dram", (1, SEQ, D), _mybir.dt.float32, kind="ExternalOutput").ap())
    build(nc, *args)
    r = _run(nc, [arrays], core_ids=[0])
    return r.results[0]["out_dram"]
```

```python
from contextlib import ExitStack

import numpy as np
import concourse.bass as bass
from concourse import mybir

F32 = mybir.dt.float32
F32R = mybir.dt.float32r
I32 = mybir.dt.int32
ALU = mybir.AluOpType
ACT = mybir.ActivationFunctionType

P = 128
SEQ = 1024
D = 1024
TT = SEQ // P
KT = D // P
DH = 64
NH = 8
IH = 4
ROT = DH // 4
HALF = ROT // 2
TOPK = min(256, SEQ // 4)
THETA = 500000.0
EPS = 1e-6
DFF = 2816
FT = DFF // P
FI = FT // 2
BANK = 512
GW = NH * DH
IDXW = IH * DH + DH + IH + NH
COL_IDX = 3 * GW
COL_FOX = COL_IDX + IH * DH + DH + IH
COL_F = COL_FOX + 3 * GW
BIG = 1e30
TAKEN = -3e38
SOFT = DH ** -0.5
CHUNK_COL = [COL_IDX, COL_FOX, COL_FOX + GW, COL_FOX + 2 * GW, 0, GW, 2 * GW]
NC = len(CHUNK_COL)
PIECES = 4
N_PROJ = NC * PIECES
N_OUT = KT
N_FFN0 = N_PROJ + N_OUT
FIRST_TOPK = TOPK // P

UNITS = 2 * NH * TT


def sel_off(t):
    return P * t * (t + 1) // 2


def proj_order():
    order = [("tile", 0, t) for t in range(TT)]
    between = {(1, m + 1): ("item", m) for m in range(IH + 1)}
    slots = [(1, 7), (2, 1), (2, 2), (2, 4), (2, 6), (3, 0)]
    between.update({slot: ("score", FIRST_TOPK + i) for i, slot in enumerate(slots)})
    between[(3, 2)] = ("forget",)
    for ch in range(1, NC):
        for t in range(TT):
            order.append(("tile", ch, t))
            if (ch, t) in between:
                order.append(between[(ch, t)])
    return order


PROJ_ORDER = proj_order()
RMAGIC = 1.5 * 2.0 ** 23
PI_IN = 3.1415925
INV_FREQ = np.float32(THETA) ** (-np.arange(0, ROT, 2, dtype=np.float32) / ROT)
TWO_PI_A = 6.28125
TWO_PI_B = float(np.float32(round((2 * np.pi - 6.28125) * 2 ** 20) / 2 ** 20))
TWO_PI_C = float(2 * np.pi - 6.28125 - round((2 * np.pi - 6.28125) * 2 ** 20) / 2 ** 20)
ROPE_STEPS = 19
EARLY_ROUNDS = 152
MOD_PER_HEAD = 3
MOD_HEADS = -(-4 * KT // MOD_PER_HEAD)
WO_HEAD = [11, 11, 12, 12, 13, 14, 14, 14]
Y_GROUPS = [(k, half) for ks in (range(KT // 2, KT), range(KT // 2)) for half in range(2) for k in ks]
ROUNDS_BETWEEN = [8, 3, 7, 6, 5]
MOD_UNITS = [13 * TT + 5, 13 * TT + 6, 13 * TT + 7, 14 * TT + 5, 14 * TT + 6]


def halves(n):
    return [(b, min(BANK, n - b)) for b in range(0, n, BANK)]


def transposes_plan():
    order = [("P", 0, part) for part in range(4)]
    for s in range(UNITS + 2):
        hd, t = divmod(s, TT)
        if s < UNITS and 1 <= t <= 4 and hd + 1 < 2 * NH:
            order.append(("P", hd + 1, t - 1))
        if s in MOD_UNITS:
            order.append(("M", MOD_UNITS.index(s)))
        if s >= 2:
            order += [("T", s - 2, b) for b in range(len(halves(P * ((s - 2) % TT + 1))))]
    return order


def build(nc, x, c, positions, ada_w, ada_b, norm_attn_g, w_in, b_forget, dsa_norm_g, fox_norm_g,
          w_out, norm_ffn_g, w_gate, w_up, w_down, final_norm_g, out):
    x, c, positions, out = x[0], c[0], positions[0], out[0]
    ada_w, ada_b, w_in, w_out = ada_w[0], ada_b[0], w_in[0], w_out[0]
    w_gate, w_up, w_down = w_gate[0], w_up[0], w_down[0]
    qkv = nc.dram_tensor("qkv_scratch", (NC - 1, SEQ, GW), F32, kind="Internal").ap()
    cum_dram = nc.dram_tensor("cum_scratch", (2, NH, SEQ), F32, kind="Internal").ap()

    plan = transposes_plan()
    group_no = {g: n for n, g in enumerate(plan)}
    key_groups = [n for n, g in enumerate(plan) if g[0] == "P" and g[2] >= 2]

    with ExitStack() as ctx:
        def sem(name):
            return ctx.enter_context(nc.semaphore(name))

        def alloc(stack, name, shape, dt=F32):
            return stack.enter_context(nc.sbuf_tensor(name, shape, dt))

        def at(kb, name, shape, dt=F32):
            with ExitStack() as s:
                if kb:
                    alloc(s, f"below_{name}", [P, int(kb * 256)])
                return alloc(s, name, shape, dt)

        ident = alloc(ctx, "ident", [P, P])
        ones = alloc(ctx, "ones", [P, P])
        posi = alloc(ctx, "posi", [P, TT], I32)
        posf = alloc(ctx, "posf", [P, TT])
        ccol = alloc(ctx, "ccol", [P, KT])
        cact = alloc(ctx, "cact", [P, KT])
        gains = alloc(ctx, "gains", [P, 3, KT])
        scaleA = alloc(ctx, "scaleA", [P, 2, KT])
        shiftB = alloc(ctx, "shiftB", [P, 2, KT])
        epsc = alloc(ctx, "epsc", [P, 1])
        stat = alloc(ctx, "stat", [P, 5, 16])
        rstd = alloc(ctx, "rstd", [P, 5, 16])
        bfor = alloc(ctx, "bfor", [P, NH])
        fg = alloc(ctx, "fg", [P, 4, NH * TT])
        rp = fg
        m8 = alloc(ctx, "m8", [P, 2, 8])

        hh = at(0, "hh", [P, KT, SEQ], F32R)
        hl = at(32, "hl", [P, KT, SEQ], F32R)
        wh = at(64, "wh", [P, 4, 2, 2 * BANK], F32R)
        wl = at(96, "wl", [P, 4, 2, 2 * BANK], F32R)
        xs = at(96, "xs", [P, TT, D])
        sel = at(128, "sel", [P, sel_off(TT)])
        tri = at(146, "tri", [P, P])
        causal = at(146.5, "causal", [P, P])
        cosT = at(147, "cosT", [P, TT, HALF])
        sinT = at(147.25, "sinT", [P, TT, HALF])
        cumq = at(147.5, "cumq", [P, NH * TT])
        raw = at(148, "raw", [P, 2, D])
        stage = at(156, "stage", [P, 2, BANK])
        acc1 = at(160, "acc1", [P, 2 * D])
        ada1 = at(168, "ada1", [P, 3, 2 * D])
        hf1 = at(192, "hf1", [P, 2, BANK])
        idxn = at(160, "idxn", [P, TT, IDXW])
        pre = at(170.5, "pre", [P, NH, TT])
        iws = at(170.75, "iws", [P, TT, IH])
        cumT = at(171, "cumT", [NH * TT, 2, P], F32R)
        ixs = at(172, "ixs", [P, 2, TT, 2, DH])
        qti = at(180, "qti", [P, IH, SEQ], F32R)
        kai = at(196, "kai", [P, SEQ], F32R)
        kbi = at(200, "kbi", [P, SEQ], F32R)
        rot = at(196, "rot", [P, 4, TT * (IH + 1) * HALF])
        O = at(0, "O", [P, TT, D])
        g1b = at(32, "g1b", [P, D])
        g2b = at(36, "g2b", [P, D])
        QT = at(40, "QT", [P, 2, SEQ], F32R)
        KA = at(48, "KA", [P, 2, SEQ], F32R)
        KB = at(56, "KB", [P, 2, SEQ], F32R)
        LP = at(64, "LP", [P, 3, SEQ])
        PT = at(76, "PT", [P, 2, SEQ])
        mod23 = at(84, "mod23", [P, 2, D])
        adat = at(92, "adat", [P, D])
        adar = at(96, "adar", [P, 2, D])
        CQ = at(104, "CQ", [P, 2, SEQ], F32R)
        CK = at(112, "CK", [P, 2, SEQ], F32R)
        strip = at(120, "strip", [P, SEQ])
        junk = at(124, "junk", [P, BANK])
        nmin = at(126, "nmin", [P, UNITS])
        sums = at(126.5, "sums", [P, UNITS])
        rinv = at(127, "rinv", [P, UNITS])
        modc = at(127.5, "modc", [P, 2 * KT])
        qs = at(172, "qs", [P, TT, 2, DH])
        kd = at(176, "kd", [P, TT, 2, DH])
        Qn = [at(180, "Qn0", [P, TT, 4 * DH]), at(148, "Qn1", [P, TT, 4 * DH])]
        Kn = [at(188, "Kn0", [P, TT, 4 * DH]), at(156, "Kn1", [P, TT, 4 * DH])]
        Vn = [at(196, "Vn0", [P, TT, 4 * DH]), at(164, "Vn1", [P, TT, 4 * DH])]
        yh = at(40, "yh", [P, KT, SEQ], F32R)
        yl = at(72, "yl", [P, KT, SEQ], F32R)
        wo = [at(kb, f"wo{k}", [P, 2, D], F32R) for k, kb in enumerate((104, 112, 180, 188, 196, 148, 156, 172))]
        hf2 = at(128, "hf2", [P, 2, BANK])
        xr = at(136, "xr", [P, 2, D])
        tmp = at(144, "tmp", [P, 2, BANK])
        raw2 = at(164, "raw2", [P, 2, D])
        sil = at(136, "sil", [P, 2, BANK])
        gf = at(140, "gf", [P, 2, BANK])
        wf = [at(kb, f"wf{j}", [P, 2, D], F32R) for j, kb in enumerate((120, 104, 112, 172, 180, 188))]
        guh = [at(196, "guh0", [P, 2, SEQ], F32R), at(156, "guh1", [P, 2, SEQ], F32R)]
        gul = [at(148, "gul0", [P, 2, SEQ], F32R), at(128, "gul1", [P, 2, SEQ], F32R)]

        def wsl(n):
            return (wh if n % 8 < 4 else wl)[:, n % 4, 0, :], (wh if n % 8 < 4 else wl)[:, n % 4, 1, :]

        PS = ctx.enter_context(nc.psum_tensor("PS", [P, 8, BANK], F32))

        small_in = sem("small_in")
        x_in = [sem(f"x_in{t}") for t in range(TT)]
        bias1_in = sem("bias1_in")
        ada_in = [sem(f"ada_in{i}") for i in range(3)]
        raw_in = [sem(f"raw_in{i}") for i in range(2)]
        stage_out = [sem(f"stage_out{i}") for i in range(2)]
        cum_out = sem("cum_out")
        qkv_in = [sem(f"qkv_in{i}") for i in range(2)]
        ckb_in = [sem(f"ckb_in{i}") for i in range(2)]
        mod_bias_in = sem("mod_bias_in")
        mod_in = [sem(f"mod_in{i}") for i in range(2)]
        xr_in = [sem(f"xr_in{i}") for i in range(2)]
        fgain_in = sem("fgain_in")
        out_done = sem("out_done")
        const_ok = sem("const_ok")
        const_st = sem("const_st")
        cact_ok = sem("cact_ok")
        pos_ok = sem("pos_ok")
        rope_st = sem("rope_st")
        rope_sin = sem("rope_sin")
        ssq_ok = sem("ssq_ok")
        root_ok = sem("root_ok")
        rstd_ok = sem("rstd_ok")
        xn_ok = sem("xn_ok")
        acc1_ok = sem("acc1_ok")
        mod1_pe = sem("mod1_pe")
        mod1_ok = sem("mod1_ok")
        nt_pe = sem("nt_pe")
        nt_act = sem("nt_act")
        nt_hi = sem("nt_hi")
        nt_lo = sem("nt_lo")
        w_begin = sem("w_begin")
        w_hi = sem("w_hi")
        w_ready = sem("w_ready")
        pj_pe = sem("pj_pe")
        pj_ev = sem("pj_ev")
        ir_st = sem("ir_st")
        ix_hi = sem("ix_hi")
        ix_ready = sem("ix_ready")
        ix_pe = sem("ix_pe")
        ix_ev = sem("ix_ev")
        ix_kb = sem("ix_kb")
        sc_pe = sem("sc_pe")
        sc_relu = sem("sc_relu")
        sc_done = sem("sc_done")
        sc_mask = sem("sc_mask")
        tk_st = sem("tk_st")
        tk_done = sem("tk_done")
        fg_v = sem("fg_v")
        fg_a = sem("fg_a")
        cum_pe = sem("cum_pe")
        cum_ev = sem("cum_ev")
        cumT_pe = sem("cumT_pe")
        cumT_ok = sem("cumT_ok")
        rope_d = sem("rope_d")
        qs_hi = sem("qs_hi")
        qs_ready = sem("qs_ready")
        kd_ready = sem("kd_ready")
        strip_ok = sem("strip_ok")
        rotated = sem("rotated")
        md_ms = sem("md_ms")
        md_a = sem("md_a")
        md_done = sem("md_done")
        qk_pe = sem("qk_pe")
        lg_done = sem("lg_done")
        ex_done = sem("ex_done")
        tp_pe = sem("tp_pe")
        tp_ev = sem("tp_ev")
        kb_ev = sem("kb_ev")
        pv_pe = sem("pv_pe")
        rv_ok = sem("rv_ok")
        on_done = sem("on_done")
        wo_in = [sem(f"wo_in{i}") for i in range(2)]
        ysum = sem("ysum")
        md_ev = sem("md_ev")
        ysq = sem("ysq")
        yroot = sem("yroot")
        yrstd = sem("yrstd")
        yn_ok = sem("yn_ok")
        yt_pe = sem("yt_pe")
        yt_act = sem("yt_act")
        yt_hi = sem("yt_hi")
        yt_lo = sem("yt_lo")
        op_pe = sem("op_pe")
        op_mul = sem("op_mul")
        x1_ok = sem("x1_ok")
        h2_root = sem("h2_root")
        h2_sq = sem("h2_sq")
        h2_rstd = sem("h2_rstd")
        h2_xn = sem("h2_xn")
        h2_pe = sem("h2_pe")
        h2_act = sem("h2_act")
        h2_hi = sem("h2_hi")
        h2_lo = sem("h2_lo")
        g_pe = sem("g_pe")
        u_pe = sem("u_pe")
        silu_ok = sem("silu_ok")
        mul_ok = sem("mul_ok")
        gu_hi = sem("gu_hi")
        gu_ready = sem("gu_ready")
        dn_pe = sem("dn_pe")
        dn_mul = sem("dn_mul")
        acc_ok = sem("acc_ok")
        fin_sq = sem("fin_sq")
        fin_root = sem("fin_root")
        fin_rstd = sem("fin_rstd")
        fin_ok = sem("fin_ok")

        raw_target = {}
        count = [0, 0]
        for n in range(N_PROJ):
            count[n % 2] += 32 if n < PIECES else 16
            raw_target[n] = count[n % 2]
        raw_base = list(count)

        SMALL = 16 * 7
        GROUPS = 2 * NH // 4

        ctx.enter_context(nc.allow_non_contiguous_dma(reason="short vectors onto partitions"))
        block = ctx.enter_context(nc.Block())

        @block.sync
        def _(sp):
            def load_piece(n):
                ch, j = divmod(n, PIECES)
                if n >= 2:
                    sp.wait_ge(w_ready, n - 1)
                w = IDXW if ch == 0 else GW
                dst = raw[:, n % 2, 0:2 * w].rearrange("p (a n) -> p a n", a=2)
                src = w_in[2 * j * P:(2 * j + 2) * P, :].rearrange("(a p) n -> p a n", p=P)
                w0 = IDXW - NH if ch == 0 else GW
                sp.dma_start(dst[:, :, 0:w0], src[:, :, CHUNK_COL[ch]:CHUNK_COL[ch] + w0]).then_inc(raw_in[n % 2], 16)
                if ch == 0:
                    sp.dma_start(dst[:, :, w0:w], src[:, :, COL_F:COL_F + NH]).then_inc(raw_in[n % 2], 16)

            def load_ada(k):
                if k >= 3:
                    sp.wait_ge(acc1_ok, k - 2)
                sp.dma_start(ada1[:, k % 3, :], ada_w[k * P:(k + 1) * P, 0:2 * D]).then_inc(ada_in[k % 3], 16)

            sp.dma_start(ccol[:], c.rearrange("(k p) -> p k", p=P)).then_inc(small_in, 16)
            sp.dma_start(posi[:], positions.rearrange("(t p) -> p t", p=P)).then_inc(small_in, 16)
            for t in range(2):
                sp.dma_start(xs[:, t, :], x[t * P:(t + 1) * P, :]).then_inc(x_in[t], 16)
            for k in range(3):
                load_ada(k)
            sp.dma_start(gains[:, 0, :], norm_attn_g[0].rearrange("(k p) -> p k", p=P)).then_inc(small_in, 16)
            sp.dma_start(gains[:, 1, 0:4], dsa_norm_g[0].rearrange("(k p) -> p k", p=P)).then_inc(small_in, 16)
            sp.dma_start(gains[:, 1, 4:8], fox_norm_g[0].rearrange("(k p) -> p k", p=P)).then_inc(small_in, 16)
            sp.dma_start(gains[:, 2, :], norm_ffn_g[0].rearrange("(k p) -> p k", p=P)).then_inc(small_in, 16)
            sp.dma_start(bfor[:], b_forget[0:1, :].to_broadcast([P, NH])).then_inc(small_in, 16)
            sp.wait_ge(const_ok, 1)
            sp.dma_start(acc1[0:1, :], ada_b[0:2 * D].rearrange("(a n) -> a n", a=1)).then_inc(bias1_in, 16)
            for k in range(3, KT):
                load_ada(k)
                t = k - 1
                sp.dma_start(xs[:, t, :], x[t * P:(t + 1) * P, :]).then_inc(x_in[t], 16)
            sp.dma_start(xs[:, TT - 1, :], x[(TT - 1) * P:, :]).then_inc(x_in[TT - 1], 16)
            for n in range(2 * PIECES):
                load_piece(n)
            def load_heads(g):
                first = 0 if g < GROUPS // 2 else 3
                cols = slice((g % 2) * 4 * DH, (g % 2 + 1) * 4 * DH)
                if g == 2:
                    sp.wait_ge(kd_ready, 4)
                    sp.wait_ge(qs_ready, 4)
                    sp.wait_ge(pv_pe, 4 * TT)
                if g == 3:
                    sp.wait_ge(kd_ready, 8)
                    sp.wait_ge(qs_ready, 8)
                    sp.wait_ge(pv_pe, 8 * TT)
                for i, dst in enumerate((Qn, Kn, Vn)):
                    src = qkv[first + i].rearrange("(t p) n -> p t n", p=P)[:, :, cols]
                    sp.dma_start(dst[g % 2][:], src).then_inc(qkv_in[g % 2], 16)

            def load_cum(hd):
                if hd >= 2:
                    sp.wait_ge(qk_pe, TT * (hd - 1))
                sp.dma_start(CK[0:2, hd % 2, :].bitcast(F32), cum_dram[:, hd, :]).then_inc(ckb_in[hd % 2], 16)
                sp.dma_start(CQ[2:4, hd % 2, :].bitcast(F32), cum_dram[:, hd, :]).then_inc(ckb_in[hd % 2], 16)

            for ch in range(1, NC):
                if ch == 5:
                    for i in range(2):
                        sp.wait_ge(stage_out[i], 16 * 3 * TT // 2)
                    sp.wait_ge(sc_pe, IH * (TT - FIRST_TOPK))
                    load_heads(0)
                if ch == 6:
                    sp.wait_ge(strip_ok, 6)
                    sp.wait_ge(cum_out, 16)
                    load_cum(0)
                    load_cum(1)
                for t in range(TT):
                    q = TT * (ch - 1) + t
                    sp.wait_ge(pj_ev, TT * ch + t + 1)
                    sp.dma_start(qkv[ch - 1, t * P:(t + 1) * P, :], stage[:, q % 2, :]).then_inc(stage_out[q % 2], 16)
                    if t < PIECES and ch + 1 < NC:
                        load_piece(PIECES * (ch + 1) + t)
                if ch == 4:
                    sp.wait_ge(cumT_ok, 2)
                    sp.dma_start(cum_dram.rearrange("a h (t p) -> (h t) a p", p=P), cumT[:].bitcast(F32)).then_inc(cum_out, 16)

            def load_mod(n):
                i, k = divmod(n, KT)
                if n >= 2:
                    sp.wait_ge(md_a, n - 1)
                sp.dma_start(adar[:, n % 2, :], ada_w[k * P:(k + 1) * P, (2 + i) * D:(3 + i) * D]).then_inc(mod_in[n % 2], 16)

            for i in range(2):
                sp.wait_ge(stage_out[i], 16 * (NC - 1) * TT // 2)
            sp.wait_ge(w_ready, N_PROJ)
            sp.wait_ge(pj_pe, NC * TT)
            load_heads(1)
            sp.wait_ge(md_ms, 3)
            for i, dst in enumerate((g1b[0:1, :], mod23[0:1, 0, :], mod23[0:1, 1, :], g2b[0:1, :])):
                sp.dma_start(dst, ada_b[(2 + i) * D:(3 + i) * D].rearrange("(a n) -> a n", a=1)).then_inc(mod_bias_in, 16)
            n_mod = 0
            for hd in range(MOD_HEADS):
                if 1 <= hd and hd + 1 < NH:
                    load_cum(hd + 1)
                if hd == 5:
                    load_heads(2)
                if hd == 9:
                    load_heads(3)
                while n_mod < min(MOD_PER_HEAD * (hd + 1), 4 * KT):
                    load_mod(n_mod)
                    n_mod += 1

            for k in range(KT):
                if k >= 2:
                    sp.wait_ge(w_ready, N_PROJ + k - 1)
                else:
                    sp.wait_ge(md_a, 4 * KT - 1 + k)
                sp.dma_start(adar[:, k % 2, :], w_out[k * P:(k + 1) * P, :]).then_inc(wo_in[k % 2], 16)

            sp.wait_ge(pv_pe, UNITS)
            for t in range(2):
                sp.dma_start(xr[:, t, :], x[t * P:(t + 1) * P, :]).then_inc(xr_in[t], 16)
            for j in range(2):
                src = (w_gate, w_up)[j][:, 0:P].rearrange("(k p) n -> p k n", p=P)
                sp.dma_start(raw2[:, j, :].rearrange("p (k n) -> p k n", k=KT), src).then_inc(raw_in[j], 16)
            for t in range(2, TT):
                sp.wait_ge(h2_pe, 2 * (t - 1))
                sp.dma_start(xr[:, t % 2, :], x[t * P:(t + 1) * P, :]).then_inc(xr_in[t % 2], 16)

            def load_gu(n, j, col):
                sp.wait_ge(w_ready, n - 1)
                src = (w_gate, w_up)[j % 2][:, bass.ds(col, P)].rearrange("(k p) n -> p k n", p=P)
                sp.dma_start(raw2[:, j % 2, :].rearrange("p (k n) -> p k n", k=KT), src).then_inc(raw_in[j % 2], 16)

            def load_down(n, j, row):
                sp.wait_ge(w_ready, n - 1)
                sp.dma_start(raw2[:, j % 2, :], w_down[bass.ds(row, P), :]).then_inc(raw_in[j % 2], 16)

            for j in (2, 3):
                load_gu(N_FFN0 + j, j, P)
            with sp.Fori(1, FI) as i:
                for j in range(4):
                    load_gu(N_FFN0 + 6 * i + j, j, (2 * i + j // 2) * P)
                for j in (4, 5):
                    load_down(N_FFN0 + 6 * i + j, j, (2 * i - 2 + j - 4) * P)
            for j in range(2):
                load_down(N_FFN0 + 6 * FI + j, j, (2 * FI - 2 + j) * P)
            sp.wait_ge(w_ready, N_FFN0 + 6 * FI + 1)
            sp.dma_start(raw2[:, 0, :],
                         final_norm_g.rearrange("(a n) -> a n", a=1).to_broadcast([P, D])).then_inc(fgain_in, 16)
            for t in range(TT):
                sp.wait_ge(fin_ok, t + 1)
                sp.dma_start(out[t * P:(t + 1) * P, :], O[:, t, :]).then_inc(out_done, 16)
            sp.wait_ge(out_done, 16 * TT)

        @block.gpsimd
        def _(pool):
            pool.memset(acc1[:], 0.0).then_inc(const_ok, 1)
            pool.memset(ident[:], 0.0).then_inc(const_st, 1)
            pool.memset(ones[:], 1.0).then_inc(const_st, 1)
            pool.memset(causal[:], BIG).then_inc(const_st, 1)
            pool.memset(epsc[:], EPS).then_inc(const_st, 1)
            pool.memset(sel[:, 0:sel_off(FIRST_TOPK)], 0.0).then_inc(const_st, 1)
            pool.wait_ge(const_st, 5)
            pool.affine_select(out=ident[:], in_=ident[:], compare_op=ALU.not_equal, fill=1.0, base=0,
                               pattern=[[-1, P]], channel_multiplier=1).then_inc(const_ok, 1)
            pool.affine_select(out=tri[:], in_=ones[:], compare_op=ALU.is_ge, fill=0.0, base=0,
                               pattern=[[1, P]], channel_multiplier=-1).then_inc(const_ok, 1)
            pool.affine_select(out=causal[:], in_=causal[:], compare_op=ALU.is_gt, fill=0.0, base=0,
                               pattern=[[1, P]], channel_multiplier=-1).then_inc(const_ok, 1)
            pool.wait_ge(const_ok, 4)
            for t in range(FIRST_TOPK):
                o = sel_off(t) + t * P
                pool.tensor_copy(sel[:, o:o + P], causal[:]).then_inc(const_ok, 1)

            def split(n, hi, lo, src, inc=1):
                pool.tensor_copy(hi, src).then_inc(w_hi, inc)
                pool.wait_ge(w_hi, n + 1)
                return pool.tensor_tensor(lo, src, hi.bitcast(F32), ALU.subtract)

            for n in range(N_PROJ):
                ch = n // PIECES
                w = IDXW if ch == 0 else GW
                pool.wait_ge(raw_in[n % 2], raw_target[n])
                if ch == 1 and n % PIECES == 0:
                    pool.wait_ge(nt_pe, 2 * KT)
                if ch >= 2:
                    pool.wait_ge(pj_pe, TT * (ch - 1))
                hi, lo = wsl(n)
                split(n, hi[:, 0:2 * w], lo[:, 0:2 * w], raw[:, n % 2, 0:2 * w]).then_inc(w_ready, 1)

            pool.wait_ge(pj_pe, (NC - 1) * TT)
            for dst, value in ((CQ, 1.0), (CK, -1.0)):
                pool.memset(dst[:].bitcast(I32), 0).then_inc(strip_ok, 1)
                pool.wait_ge(strip_ok, 1 if value > 0 else 3)
                pool.memset(dst[0:4].bitcast(F32), value).then_inc(strip_ok, 1)
            pool.memset(strip[:, 0:SEQ - P], 0.0).then_inc(strip_ok, 1)
            pool.tensor_copy(strip[:, SEQ - P:], causal[:]).then_inc(strip_ok, 1)

            steps = {"rope": 0}

            def rotary(g):
                for v in (Qn, Kn):
                    v4 = v[g % 2][:].rearrange("p t (h d) -> p t h d", d=DH)
                    x1, x2 = v4[:, :, :, 0:HALF], v4[:, :, :, HALF:ROT]
                    co = cosT[:].unsqueeze(2).to_broadcast([P, TT, 4, HALF])
                    si = sinT[:].unsqueeze(2).to_broadcast([P, TT, 4, HALF])
                    tm = [adat[:, i * 256:(i + 1) * 256].rearrange("p (t h d) -> p t h d", t=TT, h=4) for i in range(4)]
                    for dst, a, b in ((tm[0], x1, co), (tm[1], x2, si), (tm[2], x2, co), (tm[3], x1, si)):
                        pool.tensor_tensor(dst, a, b, ALU.mult).then_inc(rope_d, 1)
                    steps["rope"] += 4
                    pool.wait_ge(rope_d, steps["rope"])
                    pool.tensor_tensor(x1, tm[0], tm[1], ALU.subtract).then_inc(rope_d, 1)
                    pool.tensor_tensor(x2, tm[2], tm[3], ALU.add).then_inc(rope_d, 1)
                    steps["rope"] += 2
                    pool.wait_ge(rope_d, steps["rope"])
                pool.sem_inc(rotated, 1)

            def prepare(hd):
                g = hd // 4
                pool.wait_ge(qkv_in[g % 2], 48 * (g // 2 + 1))
                cols = slice((hd % 4) * DH, (hd % 4 + 1) * DH)
                q, k = Qn[g % 2][:, :, cols], Kn[g % 2][:, :, cols]
                if hd >= 1:
                    pool.wait_ge(tp_pe, group_no[("P", hd - 1, 3)] + 1)
                pool.tensor_copy(qs[:, :, 0, :].bitcast(F32R), q).then_inc(qs_hi, 1)
                if hd <= NH:
                    pool.tensor_copy(kd[:], k.unsqueeze(2).to_broadcast([P, TT, 2, DH])).then_inc(kd_ready, 1)
                pool.wait_ge(qs_hi, hd + 1)
                pool.tensor_tensor(qs[:, :, 1, :], q, qs[:, :, 0, :], ALU.subtract).then_inc(qs_ready, 1)

            sums_of = [g1b[:], mod23[:, 0, :], mod23[:, 1, :], g2b[:]]

            def modulation(n):
                i, k = divmod(n, KT)
                if n == 0:
                    pool.wait_ge(mod_bias_in, 64)
                pool.wait_ge(mod_in[n % 2], 16 * (n // 2 + 1))
                if n >= 1:
                    pool.wait_ge(md_done, n)
                pool.tensor_scalar(adat[:], adar[:, n % 2, :], cact[:, k:k + 1], 1.0, ALU.mult, ALU.mult).then_inc(md_a, 1)
                pool.wait_ge(md_a, n + 1)
                pool.tensor_tensor(sums_of[i], sums_of[i], adat[:], ALU.add).then_inc(md_done, 1)

            def split_out(k):
                pool.wait_ge(wo_in[k % 2], 16 * (k // 2 + 1))
                if k < 2:
                    pool.wait_ge(qk_pe, NH * TT)
                elif k in (2, 3):
                    pool.wait_ge(qs_ready, 12)
                    pool.wait_ge(kd_ready, 12)
                elif k == 4:
                    pool.wait_ge(pv_pe, 12 * TT)
                elif k in (5, 6):
                    pool.wait_ge(qs_ready, 16)
                    pool.wait_ge(kd_ready, 16)
                else:
                    pool.wait_ge(tp_pe, group_no[("P", 2 * NH - 1, 3)] + 1)
                split(N_PROJ + k, wo[k][:, 0, :], wo[k][:, 1, :], adar[:, k % 2, :]).then_inc(w_ready, 1)

            pool.wait_ge(cumT_ok, 2)
            prepare(0)
            pool.wait_ge(pj_pe, NC * TT)
            for dst in (g1b, g2b, mod23):
                pool.memset(dst[:], 0.0).then_inc(md_ms, 1)
            n_mod = 0
            for hd in range(2 * NH):
                if hd + 1 < 2 * NH:
                    if hd + 1 in (8, 12):
                        g = (hd + 1) // 4
                        pool.wait_ge(qkv_in[g % 2], 96)
                        pool.wait_ge(md_done, n_mod)
                        rotary(g)
                    prepare(hd + 1)
                while n_mod < min(MOD_PER_HEAD * (hd + 1), 4 * KT):
                    modulation(n_mod)
                    n_mod += 1
                for k in range(KT):
                    if WO_HEAD[k] == hd:
                        split_out(k)

            def split_ffn(n, j, uses, slot, inc=1):
                pool.wait_ge(raw_in[j % 2], uses)
                pool.sem_inc(w_begin, 1)
                split(n, wf[slot][:, 0, :], wf[slot][:, 1, :], raw2[:, j % 2, :], inc).then_inc(w_ready, inc)

            pool.wait_ge(md_ev, 2)
            pool.wait_ge(ysum, 3 * TT + 1)
            for j in range(4):
                if j == 1:
                    pool.wait_ge(op_pe, 2 * TT)
                split_ffn(N_FFN0 + j, j, raw_base[j % 2] + 16 * (j // 2 + 1), j, 3 if j == 3 else 1)
            with pool.Fori(1, FI) as i:
                for j in range(6):
                    if j < 4:
                        pool.wait_ge(u_pe if j % 2 else g_pe, 4 * (i - 1) + 2 * (j // 2) + 2)
                    elif j == 4:
                        pool.wait_ge(dn_pe, 16 * i)
                    split_ffn(N_FFN0 + 6 * i + j, j, raw_base[j % 2] + 32 + 48 * (i - 1) + 16 * (j // 2 + 1), j)
            for j in range(2):
                pool.wait_ge(u_pe if j else g_pe, 4 * (FI - 1) + 2)
                split_ffn(N_FFN0 + 6 * FI + j, j, raw_base[j % 2] + 32 + 48 * (FI - 1) + 16, j)

        @block.scalar
        def _(act):
            act.wait_ge(small_in, SMALL)
            act.activation(cact[:], ccol[:], ACT.Silu).then_inc(cact_ok, 1)
            act.wait_ge(rope_st, ROPE_STEPS)
            act.activation(sinT[:].rearrange("p t j -> p (t j)"), rp[:, 2, :], ACT.Sin).then_inc(rope_sin, 1)
            act.activation(cosT[:].rearrange("p t j -> p (t j)"), rp[:, 3, :], ACT.Sin).then_inc(rope_sin, 1)
            for t in range(TT):
                act.wait_ge(x_in[t], 16)
                if t >= 1:
                    act.wait_ge(ssq_ok, t)
                act.activation(PS[:, 0:2, :].rearrange("p a b -> p (a b)"), xs[:, t, :], ACT.Square,
                               accum_out=stat[:, 0, t:t + 1]).then_inc(ssq_ok, 1)
            act.wait_ge(ssq_ok, TT)
            act.wait_ge(const_ok, 4)
            act.activation(stat[:, 1, 0:TT], stat[:, 0, 0:TT], ACT.Sqrt, bias=epsc[:], scale=1.0 / D).then_inc(root_ok, 1)
            act.wait_ge(mod1_ok, 2)
            for g in range(2 * KT):
                k = g % KT
                act.wait_ge(nt_pe, g + 1)
                if g >= 2:
                    act.wait_ge(nt_lo, g - 1)
                act.activation(hh[:, k, (g // KT) * BANK:(g // KT + 1) * BANK], PS[:, 4 + g % 4, :], ACT.Identity,
                               bias=shiftB[:, 0, k:k + 1], scale=scaleA[:, 0, k:k + 1]).then_inc(nt_hi, 1)
                act.activation(hf1[:, g % 2, :], PS[:, 4 + g % 4, :], ACT.Identity, bias=shiftB[:, 0, k:k + 1],
                               scale=scaleA[:, 0, k:k + 1]).then_inc(nt_act, 1)

            def evac_tile(ch, t):
                q = TT * ch + t
                act.wait_ge(pj_pe, q + 1)
                if ch == 0:
                    if t == 0:
                        act.wait_ge(nt_lo, 2 * KT)
                    act.mul(idxn[:, t, 0:IH * DH], PS[:, q % 4, 0:IH * DH], SOFT)
                    act.copy(idxn[:, t, IH * DH:IDXW], PS[:, q % 4, IH * DH:IDXW]).then_inc(pj_ev, 1)
                    return
                n = q - TT
                if n >= 2:
                    act.wait_ge(stage_out[n % 2], 16 * (n // 2))
                act.mul(stage[:, n % 2, :], PS[:, q % 4, :], -SOFT if ch in (1, 4) else 1.0).then_inc(pj_ev, 1)

            def evac_item(m):
                for half in range(2):
                    g = 2 * m + half
                    act.wait_ge(ix_pe, g + 1)
                    cols = slice(half * BANK, (half + 1) * BANK)
                    dst = kai[:, cols] if m == 0 else qti[:, m - 1, cols]
                    act.copy(dst, PS[:, 4 + g % 4, :]).then_inc(ix_ev, 1)

            def relu_scores(t):
                n = P * (t + 1)
                for h in range(IH):
                    si = IH * (t - FIRST_TOPK) + h
                    act.wait_ge(sc_pe, si + 1)
                    b = 4 + 2 * (si % 2)
                    v = PS[:, b:b + 2, :].rearrange("p a b -> p (a b)")[:, 0:n]
                    act.activation(v, v, ACT.Relu).then_inc(sc_relu, 1)

            def forget():
                act.wait_ge(fg_v, 3)
                act.activation(fg[:, 1, :], fg[:, 1, :], ACT.Exp).then_inc(fg_a, 1)
                act.wait_ge(fg_a, 1)
                act.activation(fg[:, 1, :], fg[:, 1, :], ACT.Ln, bias=1.0).then_inc(fg_a, 1)
                act.wait_ge(cum_pe, 1)
                act.copy(cumq[:], PS[:, 4, 0:NH * TT]).then_inc(cum_ev, 1)
                act.wait_ge(cumT_pe, 1)
                act.copy(cumT[:, 0, :], PS[0:NH * TT, 5, 0:P]).then_inc(cumT_ok, 1)

            for step in PROJ_ORDER:
                if step[0] == "tile":
                    evac_tile(step[1], step[2])
                elif step[0] == "item":
                    evac_item(step[1])
                elif step[0] == "score":
                    relu_scores(step[1])
                else:
                    forget()

            def evac_group(g):
                n = group_no[g]
                act.wait_ge(tp_pe, n + 1)
                src = PS[:, 4 + n % 2, :]
                if g[0] == "P":
                    hd, part = g[1], g[2]
                    if hd >= 2:
                        act.wait_ge(qk_pe, TT * (hd - 1))
                    dst = (QT if part < 2 else KA)[:, hd % 2, (part % 2) * BANK:(part % 2 + 1) * BANK]
                    act.copy(dst, src).then_inc(tp_ev, 1)
                elif g[0] == "M":
                    i = g[1]
                    if i < 4:
                        act.copy((g1b, g2b)[i // 2][:, (i % 2) * BANK:(i % 2 + 1) * BANK], src).then_inc(tp_ev, 1)
                    else:
                        act.copy(modc[:], src[:, 0:2 * KT]).then_inc(tp_ev, 1)
                else:
                    u, b = g[1], g[2]
                    w = halves(P * (u % TT + 1))[b][1]
                    if u >= 2 and b == 0:
                        act.wait_ge(pv_pe, u - 1)
                    act.copy(PT[:, u % 2, b * BANK:b * BANK + w], src[:, 0:w]).then_inc(tp_ev, 1)

            def expo(u):
                n = P * (u % TT + 1)
                act.wait_ge(lg_done, u + 1)
                act.activation(LP[:, u % 3, 0:n], LP[:, u % 3, 0:n], ACT.Exp, bias=nmin[:, u:u + 1], scale=-1.0,
                               accum_out=sums[:, u:u + 1]).then_inc(ex_done, 1)

            def roots(kind):
                act.wait_ge(ysum, TT if kind else 3 * TT + 1)
                act.activation(stat[:, 3, kind * TT:(kind + 1) * TT], stat[:, 2, kind * TT:(kind + 1) * TT], ACT.Sqrt,
                               bias=epsc[:], scale=1.0 / GW).then_inc(yroot, 1)

            for part in range(4):
                evac_group(("P", 0, part))
            for s in range(UNITS + 2):
                hd, t = divmod(s, TT)
                if s < UNITS and 1 <= t <= 4 and hd + 1 < 2 * NH:
                    evac_group(("P", hd + 1, t - 1))
                if s in MOD_UNITS:
                    evac_group(("M", MOD_UNITS.index(s)))
                if s == 11 * TT:
                    roots(1)
                if s >= 2:
                    for b in range(len(halves(P * ((s - 2) % TT + 1)))):
                        evac_group(("T", s - 2, b))
                if s < UNITS:
                    expo(s)

            roots(0)
            act.wait_ge(w_ready, N_FFN0)
            for g, (k, half) in enumerate(Y_GROUPS):
                cols = slice(half * BANK, (half + 1) * BANK)
                act.wait_ge(yt_pe, g + 1)
                act.activation(yh[:, k, cols], PS[:, 4 + g % 4, :], ACT.Identity, scale=gains[:, 1, k:k + 1]).then_inc(yt_hi, 1)
                if g >= 2:
                    act.wait_ge(yt_lo, g - 1)
                act.activation(hf2[:, g % 2, :], PS[:, 4 + g % 4, :], ACT.Identity,
                               scale=gains[:, 1, k:k + 1]).then_inc(yt_act, 1)

            def root2(t):
                act.wait_ge(x1_ok, 2 * t + 2)
                act.activation(PS[:, 4:6, :].rearrange("p a b -> p (a b)"), O[:, t, :], ACT.Square,
                               accum_out=stat[:, 0, t:t + 1]).then_inc(h2_sq, 1)
                act.wait_ge(h2_sq, t + 1)
                act.activation(stat[:, 1, t:t + 1], stat[:, 0, t:t + 1], ACT.Sqrt, bias=epsc[:],
                               scale=1.0 / D).then_inc(h2_root, 1)

            def scale2(t):
                for kh in range(2):
                    g = 2 * t + kh
                    act.wait_ge(h2_pe, g + 1)
                    if g >= 2:
                        act.wait_ge(h2_lo, g - 1)
                    for i in range(4):
                        k = 4 * kh + i
                        last = act.activation(hf2[:, g % 2, i * P:(i + 1) * P], PS[:, 6 + g % 2, i * P:(i + 1) * P],
                                              ACT.Identity, bias=shiftB[:, 1, k:k + 1], scale=scaleA[:, 1, k:k + 1])
                    last.then_inc(h2_act, 1)

            act.wait_ge(yt_lo, 2 * KT)
            for s in range(TT + 2):
                if s < TT:
                    root2(s)
                if s >= 2:
                    scale2(s - 2)

            def gated(i, par, first=False):
                for a in range(2):
                    for hf in range(2):
                        idx = 4 * i + 2 * a + hf
                        act.wait_ge(g_pe, idx + 1)
                        if not (first and a == 0):
                            act.wait_ge(mul_ok, idx - 1)
                        act.activation(sil[:, hf, :], PS[:, hf, :], ACT.Silu).then_inc(silu_ok, 1)
                    for hf in range(2):
                        idx = 4 * i + 2 * a + hf
                        act.wait_ge(mul_ok, idx + 1)
                        act.copy(guh[par][:, a, hf * BANK:(hf + 1) * BANK], gf[:, hf, :]).then_inc(gu_hi, 1)

            gated(0, 0, True)
            with act.Fori(1, FI, 2) as i0:
                for odd in range(2):
                    i = i0 + odd
                    act.wait_ge(dn_pe, 16 * i)
                    gated(i, 1 - odd)
            for t in range(TT):
                act.wait_ge(acc_ok, 16 * FI + 2 * t + 2)
                act.activation(PS[:, 0:2, :].rearrange("p a b -> p (a b)"), O[:, t, :], ACT.Square,
                               accum_out=stat[:, 0, t:t + 1]).then_inc(fin_sq, 1)
                act.wait_ge(fin_sq, t + 1)
                act.activation(stat[:, 1, t:t + 1], stat[:, 0, t:t + 1], ACT.Sqrt, bias=epsc[:],
                               scale=1.0 / D).then_inc(fin_root, 1)

        @block.vector
        def _(dve):
            ang, turns, red, red2 = (rp[:, i, :] for i in range(4))
            n_rope = 0

            def rope_step(ins):
                nonlocal n_rope
                n_rope += 1
                ins.then_inc(rope_st, 1)
                dve.wait_ge(rope_st, n_rope)

            dve.wait_ge(small_in, SMALL)
            rope_step(dve.tensor_copy(posf[:], posi[:]))
            for j in range(HALF):
                rope_step(dve.tensor_scalar(ang.rearrange("p (t j) -> p t j", t=TT)[:, :, j], posf[:],
                                            float(INV_FREQ[j]), None, ALU.mult))
            rope_step(dve.tensor_scalar(turns, ang, 1.0 / (2 * np.pi), RMAGIC, ALU.mult, ALU.add))
            rope_step(dve.tensor_scalar(turns, turns, -RMAGIC, None, ALU.add))
            rope_step(dve.scalar_tensor_tensor(out=red, in0=turns, scalar=-TWO_PI_A, in1=ang, op0=ALU.mult, op1=ALU.add))
            rope_step(dve.scalar_tensor_tensor(out=red, in0=turns, scalar=-TWO_PI_B, in1=red, op0=ALU.mult, op1=ALU.add))
            rope_step(dve.scalar_tensor_tensor(out=red, in0=turns, scalar=-TWO_PI_C, in1=red, op0=ALU.mult, op1=ALU.add))
            rope_step(dve.tensor_scalar(red, red, PI_IN, -PI_IN, ALU.min, ALU.max))
            rope_step(dve.tensor_scalar(red2, red, np.pi / 2, None, ALU.add))
            rope_step(dve.tensor_scalar(turns, red2, PI_IN, -2 * np.pi, ALU.is_gt, ALU.mult))
            rope_step(dve.tensor_tensor(red2, red2, turns, ALU.add))
            rope_step(dve.tensor_scalar(red2, red2, PI_IN, -PI_IN, ALU.min, ALU.max))
            assert n_rope == ROPE_STEPS

            dve.wait_ge(cact_ok, 1)
            dve.wait_ge(bias1_in, 16)
            for k in range(KT):
                dve.wait_ge(ada_in[k % 3], 16 * (k // 3 + 1))
                if k >= 1:
                    dve.wait_ge(acc1_ok, k)
                dve.scalar_tensor_tensor(out=acc1[:], in0=ada1[:, k % 3, :], scalar=cact[:, k:k + 1], in1=acc1[:],
                                         op0=ALU.mult, op1=ALU.add).then_inc(acc1_ok, 1)
            dve.wait_ge(root_ok, 1)
            dve.reciprocal(rstd[:, 0, 0:TT], stat[:, 1, 0:TT]).then_inc(rstd_ok, 1)
            dve.wait_ge(rstd_ok, 1)
            for t in range(TT):
                dve.tensor_scalar(xs[:, t, :], xs[:, t, :], rstd[:, 0, t:t + 1], None, ALU.mult).then_inc(xn_ok, 1)
            dve.wait_ge(mod1_pe, 1)
            dve.tensor_copy(shiftB[:, 0, :], PS[:, 2, 0:KT]).then_inc(mod1_ok, 1)
            dve.scalar_tensor_tensor(out=scaleA[:, 0, :], in0=PS[:, 2, KT:2 * KT], scalar=1.0, in1=gains[:, 0, :],
                                     op0=ALU.add, op1=ALU.mult).then_inc(mod1_ok, 1)
            for g in range(2 * KT):
                k, half = g % KT, g // KT
                cols = slice(half * BANK, (half + 1) * BANK)
                dve.wait_ge(nt_act, g + 1)
                dve.wait_ge(nt_hi, g + 1)
                dve.tensor_tensor(hl[:, k, cols], hf1[:, g % 2, :], hh[:, k, cols].bitcast(F32), ALU.subtract).then_inc(nt_lo, 1)

            dve.wait_ge(pj_ev, TT)
            dve.wait_ge(rope_sin, 2)
            v4 = idxn[:, :, 0:(IH + 1) * DH].rearrange("p t (h d) -> p t h d", d=DH)
            x1, x2 = v4[:, :, :, 0:HALF], v4[:, :, :, HALF:ROT]
            co = cosT[:].unsqueeze(2).to_broadcast([P, TT, IH + 1, HALF])
            si = sinT[:].unsqueeze(2).to_broadcast([P, TT, IH + 1, HALF])
            tm = [rot[:, i, :].rearrange("p (t h d) -> p t h d", t=TT, h=IH + 1) for i in range(4)]
            for dst, a, b in ((tm[0], x1, co), (tm[1], x2, si), (tm[2], x2, co), (tm[3], x1, si)):
                dve.tensor_tensor(dst, a, b, ALU.mult).then_inc(ir_st, 1)
            dve.wait_ge(ir_st, 4)
            dve.tensor_tensor(x1, tm[0], tm[1], ALU.subtract).then_inc(ir_st, 1)
            dve.tensor_tensor(x2, tm[2], tm[3], ALU.add).then_inc(ir_st, 1)
            dve.tensor_scalar(iws[:], idxn[:, :, (IH + 1) * DH:(IH + 1) * DH + IH], IH ** -0.5, None,
                              ALU.mult).then_inc(ir_st, 1)
            dve.wait_ge(ir_st, 7)

            def index_item(m):
                if m >= 2:
                    dve.wait_ge(ix_pe, 2 * (m - 1))
                if m == 0:
                    k = idxn[:, :, IH * DH:(IH + 1) * DH]
                    dve.tensor_copy(ixs[:, 0], k.unsqueeze(2).to_broadcast([P, TT, 2, DH])).then_inc(ix_ready, 1)
                    return
                q = idxn[:, :, (m - 1) * DH:m * DH]
                dve.tensor_copy(ixs[:, m % 2, :, 0, :].bitcast(F32R), q).then_inc(ix_hi, 1)
                dve.wait_ge(ix_hi, m)
                dve.tensor_tensor(ixs[:, m % 2, :, 1, :], q, ixs[:, m % 2, :, 0, :], ALU.subtract).then_inc(ix_ready, 1)

            index_item(0)
            index_item(1)
            for half in range(2):
                cols = slice(half * BANK, (half + 1) * BANK)
                dve.wait_ge(ix_ev, half + 1)
                dve.tensor_tensor(kbi[:, cols], PS[:, 4 + half, :], kai[:, cols].bitcast(F32), ALU.subtract).then_inc(ix_kb, 1)
            for m in range(2, IH + 1):
                index_item(m)

            fht = [fg[:, i, :].rearrange("p (h t) -> p h t", h=NH) for i in range(4)]
            dve.tensor_tensor(fht[0], idxn[:, :, IDXW - NH:IDXW].rearrange("p t h -> p h t"),
                              bfor[:].unsqueeze(2).to_broadcast([P, NH, TT]), ALU.add).then_inc(fg_v, 1)
            dve.wait_ge(fg_v, 1)
            dve.tensor_scalar(fg[:, 2, :], fg[:, 0, :], 0.0, None, ALU.min).then_inc(fg_v, 1)
            dve.scalar_tensor_tensor(out=fg[:, 1, :], in0=fg[:, 0, :], scalar=-1.0, in1=fg[:, 0, :],
                                     op0=ALU.mult, op1=ALU.min).then_inc(fg_v, 1)

            n_sc = 0

            def score(t):
                nonlocal n_sc
                n = P * (t + 1)
                o = sel_off(t)
                for h in range(IH):
                    dve.wait_ge(sc_relu, n_sc + 1)
                    b = 4 + 2 * (n_sc % 2)
                    v = PS[:, b:b + 2, :].rearrange("p a b -> p (a b)")[:, 0:n]
                    w = iws[:, t, h:h + 1]
                    if h == 0:
                        dve.tensor_scalar(sel[:, o:o + n], v, w, None, ALU.mult).then_inc(sc_done, 1)
                    else:
                        dve.wait_ge(sc_done, n_sc)
                        dve.scalar_tensor_tensor(out=sel[:, o:o + n], in0=v, scalar=w, in1=sel[:, o:o + n],
                                                 op0=ALU.mult, op1=ALU.add).then_inc(sc_done, 1)
                    n_sc += 1
                dve.wait_ge(sc_done, n_sc)
                dve.tensor_tensor(sel[:, o + n - P:o + n], sel[:, o + n - P:o + n], causal[:],
                                  ALU.subtract).then_inc(sc_mask, 1)

            ROUNDS = TOPK // 8
            all_rounds = [(t, r) for t in range(FIRST_TOPK, TT) for r in range(ROUNDS)]
            n_tk = 0
            n_round = 0

            def rounds(count):
                nonlocal n_tk, n_round
                for t, r in all_rounds[n_round:n_round + count]:
                    v = sel[:, sel_off(t):sel_off(t + 1)]
                    if n_tk:
                        dve.wait_ge(tk_st, n_tk)
                    if r == 0:
                        dve.wait_ge(sc_mask, t - FIRST_TOPK + 1)
                    dve.max(m8[:, r % 2, :], v).then_inc(tk_st, 1)
                    dve.wait_ge(tk_st, n_tk + 1)
                    dve.match_replace(v, m8[:, r % 2, :], v, TAKEN).then_inc(tk_st, 1)
                    n_tk += 2
                    if r == ROUNDS - 1:
                        dve.wait_ge(tk_st, n_tk)
                        dve.tensor_scalar(v, v, TAKEN / 1.5, BIG, ALU.is_ge, ALU.mult).then_inc(tk_done, 1)
                n_round += count

            for t in range(FIRST_TOPK, TT):
                score(t)
                if t < TT - 1:
                    rounds(ROUNDS_BETWEEN[t - FIRST_TOPK])
            dve.wait_ge(fg_a, 2)
            dve.tensor_tensor(fg[:, 3, :], fg[:, 2, :], fg[:, 1, :], ALU.subtract).then_inc(fg_v, 1)
            dve.memset(pre[:, :, 0], 0.0).then_inc(fg_v, 1)
            for t in range(1, TT):
                dve.wait_ge(fg_v, 4 + t)
                dve.tensor_tensor(pre[:, :, t], pre[:, :, t - 1], fht[3][:, :, t - 1], ALU.add).then_inc(fg_v, 1)
            dve.wait_ge(cumT_pe, 1)
            dve.wait_ge(cumT_ok, 1)
            dve.tensor_tensor(cumT[:, 1, :], PS[0:NH * TT, 5, 0:P], cumT[:, 0, :].bitcast(F32), ALU.subtract).then_inc(cumT_ok, 1)
            rounds(EARLY_ROUNDS - n_round)

            def biased(u):
                hd, t = divmod(u, TT)
                n = P * (t + 1)
                if u >= 3:
                    last = len(halves(P * ((u - 3) % TT + 1))) - 1
                    dve.wait_ge(tp_pe, group_no[("T", u - 3, last)] + 1)
                if hd < NH:
                    dve.wait_ge(strip_ok, 6)
                    bias = strip[:, SEQ - n:]
                else:
                    if t >= FIRST_TOPK:
                        dve.wait_ge(tk_done, t - FIRST_TOPK + 1)
                    bias = sel[:, sel_off(t):sel_off(t + 1)]
                dve.wait_ge(qk_pe, u + 1)
                b = 2 * (u % 2)
                v = PS[:, b:b + 2, :].rearrange("p a b -> p (a b)")[:, 0:n]
                dve.tensor_tensor_reduce(out=LP[:, u % 3, 0:n], in0=v, in1=bias, scale=1.0, scalar=3e38,
                                         op0=ALU.add, op1=ALU.min, accum_out=nmin[:, u:u + 1]).then_inc(lg_done, 1)

            def key_lo(hd, part):
                n = group_no[("P", hd, part)]
                cols = slice((part % 2) * BANK, (part % 2 + 1) * BANK)
                dve.wait_ge(tp_ev, n + 1)
                dve.tensor_tensor(KB[:, hd % 2, cols], PS[:, 4 + n % 2, :], KA[:, hd % 2, cols].bitcast(F32),
                                  ALU.subtract).then_inc(kb_ev, 1)

            def normalise(hd):
                col = GW + hd * DH if hd < NH else (hd - NH) * DH
                units = slice(hd * TT, (hd + 1) * TT)
                dve.wait_ge(pv_pe, (hd + 1) * TT)
                dve.reciprocal(rinv[:, units], sums[:, units]).then_inc(rv_ok, 1)
                dve.wait_ge(rv_ok, hd + 1)
                dve.tensor_tensor(O[:, :, col:col + DH], PS[:, 6 + hd % 2, :].rearrange("p (t d) -> p t d", t=TT),
                                  rinv[:, units].unsqueeze(2).to_broadcast([P, TT, DH]), ALU.mult).then_inc(on_done, 1)

            def twice(hd):
                g = hd // 4
                dve.wait_ge(rotated, g - 1)
                dve.wait_ge(tp_pe, group_no[("P", hd - 1, 3)] + 1)
                k = Kn[g % 2][:, :, (hd % 4) * DH:(hd % 4 + 1) * DH]
                dve.tensor_copy(kd[:], k.unsqueeze(2).to_broadcast([P, TT, 2, DH])).then_inc(kd_ready, 1)

            def square(t, col, width, part):
                if part != (1, 0) or t:
                    dve.wait_ge(ysum, n_sq[0])
                v = O[:, t, col:col + width]
                dve.tensor_tensor_reduce(out=junk[:, 0:width], in0=v, in1=v, scale=1.0, scalar=0.0, op0=ALU.mult,
                                         op1=ALU.add, accum_out=stat[:, part[0], part[1] * TT + t:part[1] * TT + t + 1]
                                         ).then_inc(ysum, 1)
                n_sq[0] += 1

            n_sq = [0]

            def scaled(t, kind):
                v = O[:, t, kind * GW:(kind + 1) * GW]
                r = kind * TT + t
                dve.tensor_scalar(v, v, rstd[:, 1, r:r + 1], None, ALU.mult).then_inc(yn_ok, 1)

            LATE = 2 * DH
            key_lo(0, 2)
            key_lo(0, 3)
            for s in range(UNITS):
                hd, t = divmod(s, TT)
                if t == 0 and NH <= hd < 2 * NH - 1:
                    twice(hd + 1)
                if hd == 10:
                    square(t, GW, GW, (2, 1))
                if hd == 11 and t == 2:
                    dve.wait_ge(yroot, 1)
                    dve.reciprocal(rstd[:, 1, TT:2 * TT], stat[:, 3, TT:2 * TT]).then_inc(yrstd, 1)
                    dve.wait_ge(yrstd, 1)
                if hd == 12:
                    scaled(t, 1)
                if hd == 15:
                    if t == 0:
                        dve.wait_ge(on_done, 2 * NH - 2)
                    square(t, 0, GW - LATE, (2, 0))
                if t in (3, 4) and hd + 1 < 2 * NH:
                    key_lo(hd + 1, t - 1)
                biased(s)
                if t == 3 and hd >= 1:
                    normalise(hd - 1)
                if t >= 3 and n_round < len(all_rounds):
                    rounds(1)
            normalise(2 * NH - 1)
            dve.wait_ge(on_done, 2 * NH)
            for t in range(TT):
                square(t, GW - LATE, LATE, (4, 0))
            dve.wait_ge(ysum, n_sq[0])
            dve.tensor_tensor(stat[:, 2, 0:TT], stat[:, 2, 0:TT], stat[:, 4, 0:TT], ALU.add).then_inc(ysum, 1)

            dve.wait_ge(tp_ev, group_no[("M", 4)] + 1)
            dve.tensor_copy(shiftB[:, 1, :], modc[:, 0:KT]).then_inc(md_ev, 1)
            dve.scalar_tensor_tensor(out=scaleA[:, 1, :], in0=modc[:, KT:2 * KT], scalar=1.0, in1=gains[:, 2, :],
                                     op0=ALU.add, op1=ALU.mult).then_inc(md_ev, 1)
            dve.wait_ge(yroot, 2)
            dve.reciprocal(rstd[:, 1, 0:TT], stat[:, 3, 0:TT]).then_inc(yrstd, 1)
            dve.wait_ge(yrstd, 2)
            for t in range(TT):
                scaled(t, 0)
            for g, (k, half) in enumerate(Y_GROUPS):
                cols = slice(half * BANK, (half + 1) * BANK)
                dve.wait_ge(yt_act, g + 1)
                dve.wait_ge(yt_hi, g + 1)
                dve.tensor_tensor(yl[:, k, cols], hf2[:, g % 2, :], yh[:, k, cols].bitcast(F32), ALU.subtract).then_inc(yt_lo, 1)

            dve.wait_ge(md_ev, 2)
            for s in range(TT + 2):
                if s < TT:
                    t = s
                    dve.wait_ge(xr_in[t % 2], 16 * (t // 2 + 1))
                    for nh in range(2):
                        q = 2 * t + nh
                        cols = slice(nh * BANK, (nh + 1) * BANK)
                        dve.wait_ge(op_pe, q + 1)
                        dve.tensor_tensor(tmp[:, q % 2, :], PS[:, q % 4, :], g1b[:, cols], ALU.mult).then_inc(op_mul, 1)
                        dve.wait_ge(op_mul, q + 1)
                        dve.tensor_tensor(O[:, t, cols], tmp[:, q % 2, :], xr[:, t % 2, cols], ALU.add).then_inc(x1_ok, 1)
                    dve.wait_ge(h2_root, t + 1)
                    dve.reciprocal(rstd[:, 2, t:t + 1], stat[:, 1, t:t + 1]).then_inc(h2_rstd, 1)
                    dve.wait_ge(h2_rstd, t + 1)
                    dve.tensor_scalar(xr[:, t % 2, :], O[:, t, :], rstd[:, 2, t:t + 1], None, ALU.mult).then_inc(h2_xn, 1)
                if s >= 2:
                    t = s - 2
                    for kh in range(2):
                        g = 2 * t + kh
                        dst = (slice(None), slice(4 * kh, 4 * kh + 4), slice(t * P, (t + 1) * P))
                        src = hf2[:, g % 2, :].rearrange("p (k n) -> p k n", k=4)
                        dve.wait_ge(h2_act, g + 1)
                        dve.tensor_copy(yh[dst], src).then_inc(h2_hi, 1)
                        dve.wait_ge(h2_hi, g + 1)
                        dve.tensor_tensor(yl[dst], src, yh[dst].bitcast(F32), ALU.subtract).then_inc(h2_lo, 1)

            def gated(i, par, first=False):
                for a in range(2):
                    for hf in range(2):
                        idx = 4 * i + 2 * a + hf
                        dve.wait_ge(silu_ok, idx + 1)
                        dve.wait_ge(u_pe, idx + 1)
                        if not (first and a == 0):
                            dve.wait_ge(gu_ready, idx - 1)
                        dve.tensor_tensor(gf[:, hf, :], PS[:, 2 + hf, :], sil[:, hf, :], ALU.mult).then_inc(mul_ok, 1)
                    for hf in range(2):
                        idx = 4 * i + 2 * a + hf
                        cols = slice(hf * BANK, (hf + 1) * BANK)
                        dve.wait_ge(gu_hi, idx + 1)
                        dve.tensor_tensor(gul[par][:, a, cols], gf[:, hf, :], guh[par][:, a, cols].bitcast(F32),
                                          ALU.subtract).then_inc(gu_ready, 1)

            def gather(i):
                for r in range(16):
                    q = 16 * i + r
                    t, nh = divmod(r, 2)
                    cols = slice(nh * BANK, (nh + 1) * BANK)
                    dve.wait_ge(dn_pe, 16 + q + 1)
                    dve.tensor_tensor(tmp[:, r % 2, :], PS[:, 4 + r % 4, :], g2b[:, cols], ALU.mult).then_inc(dn_mul, 1)
                    dve.wait_ge(dn_mul, q + 1)
                    dve.tensor_tensor(O[:, t, cols], tmp[:, r % 2, :], O[:, t, cols], ALU.add).then_inc(acc_ok, 1)

            dve.sem_inc(acc_ok, 16)
            gated(0, 0, True)
            with dve.Fori(1, FI, 2) as i0:
                for odd in range(2):
                    gated(i0 + odd, 1 - odd)
                    gather(i0 + odd - 1)
            gather(FI - 1)
            dve.wait_ge(fgain_in, 16)
            for t in range(TT):
                dve.wait_ge(fin_root, t + 1)
                dve.reciprocal(rstd[:, 3, t:t + 1], stat[:, 1, t:t + 1]).then_inc(fin_rstd, 1)
                dve.wait_ge(fin_rstd, t + 1)
                dve.scalar_tensor_tensor(out=O[:, t, :], in0=O[:, t, :], scalar=rstd[:, 3, t:t + 1],
                                         in1=raw2[:, 0, :], op0=ALU.mult, op1=ALU.mult).then_inc(fin_ok, 1)

        @block.tensor
        def _(pe):
            def three(dst, left, right, first, last):
                pe.matmul(dst, left[0], right[0], start=first, stop=False)
                pe.matmul(dst, left[0], right[1], start=False, stop=False)
                return pe.matmul(dst, left[1], right[0], start=False, stop=last)

            pe.wait_ge(const_ok, 4)
            pe.wait_ge(acc1_ok, KT)
            for j in range(2 * KT):
                last = pe.matmul(PS[:, 2, j:j + 1], acc1[:, j * P:(j + 1) * P], ones[:, 0:1], start=True, stop=True)
            last.then_inc(mod1_pe, 1)
            for g in range(2 * KT):
                k, half = g % KT, g // KT
                pe.wait_ge(xn_ok, 4 * (half + 1))
                if g >= 4:
                    pe.wait_ge(nt_act, g - 3)
                for i in range(4):
                    last = pe.transpose(PS[:, 4 + g % 4, i * P:(i + 1) * P], xs[:, 4 * half + i, k * P:(k + 1) * P], ident[:])
                last.then_inc(nt_pe, 1)

            def tile(ch, t):
                q = TT * ch + t
                w = IDXW if ch == 0 else GW
                if ch == 0:
                    pe.wait_ge(nt_lo, KT * (t // 4 + 1))
                if q >= 4:
                    pe.wait_ge(pj_ev, q - 3)
                for k in range(KT):
                    n = PIECES * ch + k // 2
                    if t == 0 and k % 2 == 0:
                        pe.wait_ge(w_ready, n + 1)
                    cols = slice((k % 2) * w, (k % 2 + 1) * w)
                    hi, lo = wsl(n)
                    rows = slice(t * P, (t + 1) * P)
                    last = three(PS[:, q % 4, 0:w], (hh[:, k, rows], hl[:, k, rows]), (hi[:, cols], lo[:, cols]),
                                 k == 0, k == KT - 1)
                last.then_inc(pj_pe, 1)

            def item(m):
                for half in range(2):
                    g = 2 * m + half
                    pe.wait_ge(ix_ready, m + 1)
                    if g >= 4:
                        pe.wait_ge(ix_ev, g - 3)
                        pe.wait_ge(ix_kb, 2)
                    for i in range(4):
                        src = ixs[:, m % 2, 4 * half + i, :, :].rearrange("p a d -> p (a d)")
                        last = pe.transpose(PS[:, 4 + g % 4, i * P:(i + 1) * P], src, ident[:])
                    last.then_inc(ix_pe, 1)

            def index_scores(t):
                n = P * (t + 1)
                for h in range(IH):
                    si = IH * (t - FIRST_TOPK) + h
                    if si < 2:
                        pe.wait_ge(ix_ev, 2 * (IH + 1))
                        pe.wait_ge(ix_kb, 2)
                    else:
                        pe.wait_ge(sc_done, si - 1)
                    q = qti[:, h, t * P:(t + 1) * P]
                    for b, w in halves(n):
                        dst = PS[:, 4 + 2 * (si % 2) + b // BANK, 0:w]
                        pe.matmul(dst, q, kai[:, b:b + w], start=True, stop=False)
                        last = pe.matmul(dst, q, kbi[:, b:b + w], start=False, stop=True)
                    last.then_inc(sc_pe, 1)

            def cumulative():
                pe.wait_ge(sc_done, IH * (TT - FIRST_TOPK))
                pe.wait_ge(fg_v, 4 + TT)
                pe.matmul(PS[:, 4, 0:NH * TT], tri[:], fg[:, 3, :], start=True, stop=False)
                pe.matmul(PS[:, 4, 0:NH * TT], ones[:], pre[:].rearrange("p h t -> p (h t)"), start=False,
                          stop=True).then_inc(cum_pe, 1)
                pe.wait_ge(cum_ev, 1)
                pe.transpose(PS[0:NH * TT, 5, 0:P], cumq[:], ident[:]).then_inc(cumT_pe, 1)

            for step in PROJ_ORDER:
                if step[0] == "tile":
                    tile(step[1], step[2])
                elif step[0] == "item":
                    item(step[1])
                elif step[0] == "score":
                    index_scores(step[1])
                else:
                    cumulative()

            def turn(g):
                n = group_no[g]
                if n >= 2:
                    pe.wait_ge(tp_ev, n - 1)
                    if n - 2 in key_groups:
                        pe.wait_ge(kb_ev, key_groups.index(n - 2) + 1)
                dst = PS[:, 4 + n % 2, :]
                if g[0] == "M":
                    i = g[1]
                    pe.wait_ge(md_done, 4 * KT)
                    if i < 4:
                        src = (g1b, g2b)[i // 2][:, (i % 2) * BANK:(i % 2 + 1) * BANK]
                        pe.matmul(dst, ones[:], src, start=True, stop=True).then_inc(tp_pe, 1)
                        return
                    for j in range(2 * KT):
                        last = pe.matmul(dst[:, j:j + 1], mod23[:, j // KT, (j % KT) * P:(j % KT + 1) * P], ones[:, 0:1],
                                         start=True, stop=True)
                    last.then_inc(tp_pe, 1)
                    return
                if g[0] == "P":
                    hd, part = g[1], g[2]
                    pe.wait_ge(qs_ready if part < 2 else kd_ready, hd + 1)
                    srcs = [(qs if part < 2 else kd)[:, 4 * (part % 2) + i, :, :].rearrange("p a d -> p (a d)") for i in range(4)]
                else:
                    u, b = g[1], g[2]
                    pe.wait_ge(ex_done, u + 1)
                    first, w = halves(P * (u % TT + 1))[b]
                    srcs = [LP[:, u % 3, first + i * P:first + (i + 1) * P] for i in range(w // P)]
                for i, src in enumerate(srcs):
                    last = pe.transpose(dst[:, i * P:(i + 1) * P], src, ident[:])
                last.then_inc(tp_pe, 1)

            def logits(u):
                hd, t = divmod(u, TT)
                if t == 0:
                    pe.wait_ge(tp_ev, group_no[("P", hd, 3)] + 1)
                    pe.wait_ge(kb_ev, 2 * (hd + 1))
                    if hd < NH:
                        pe.wait_ge(ckb_in[hd % 2], 32 * (hd // 2 + 1))
                if u >= 2:
                    pe.wait_ge(lg_done, u - 1)
                q = QT[:, hd % 2, t * P:(t + 1) * P]
                for b, w in halves(P * (t + 1)):
                    dst = PS[:, 2 * (u % 2) + b // BANK, 0:w]
                    if hd < NH:
                        pe.matmul(dst, CQ[:, hd % 2, t * P:(t + 1) * P], CK[:, hd % 2, b:b + w], start=True, stop=False)
                    pe.matmul(dst, q, KA[:, hd % 2, b:b + w], start=hd >= NH, stop=False)
                    last = pe.matmul(dst, q, KB[:, hd % 2, b:b + w], start=False, stop=True)
                last.then_inc(qk_pe, 1)

            def values(u):
                hd, t = divmod(u, TT)
                pe.wait_ge(tp_ev, group_no[("T", u, len(halves(P * (t + 1))) - 1)] + 1)
                if t == 0:
                    pe.wait_ge(qkv_in[(hd // 4) % 2], 48 * (hd // 8 + 1))
                    if hd >= 2:
                        pe.wait_ge(on_done, hd - 1)
                cols = slice((hd % 4) * DH, (hd % 4 + 1) * DH)
                for j in range(t + 1):
                    last = pe.matmul(PS[:, 6 + hd % 2, t * DH:(t + 1) * DH], PT[:, u % 2, j * P:(j + 1) * P],
                                     Vn[(hd // 4) % 2][:, j, cols], start=j == 0, stop=j == t)
                last.then_inc(pv_pe, 1)

            pe.wait_ge(pj_ev, NC * TT)
            pe.wait_ge(cumT_ok, 2)
            for part in range(4):
                turn(("P", 0, part))
            for s in range(UNITS + 3):
                hd, t = divmod(s, TT)
                if s < UNITS:
                    logits(s)
                if s < UNITS and 1 <= t <= 4 and hd + 1 < 2 * NH:
                    turn(("P", hd + 1, t - 1))
                if s in MOD_UNITS:
                    turn(("M", MOD_UNITS.index(s)))
                if 2 <= s < UNITS + 2:
                    for b in range(len(halves(P * ((s - 2) % TT + 1)))):
                        turn(("T", s - 2, b))
                if s >= 3:
                    values(s - 3)

            pe.wait_ge(tp_ev, len(plan))
            for g, (k, half) in enumerate(Y_GROUPS):
                pe.wait_ge(yn_ok, TT if k >= KT // 2 else TT + 4 * (half + 1))
                if g == 2:
                    pe.wait_ge(on_done, 2 * NH)
                if g >= 4:
                    pe.wait_ge(yt_act, g - 3)
                for i in range(4):
                    last = pe.transpose(PS[:, 4 + g % 4, i * P:(i + 1) * P], O[:, 4 * half + i, k * P:(k + 1) * P], ident[:])
                last.then_inc(yt_pe, 1)

            def turn2(t):
                pe.wait_ge(h2_xn, t + 1)
                if t == 0:
                    pe.wait_ge(yt_act, 2 * KT)
                for kh in range(2):
                    g = 2 * t + kh
                    if g >= 2:
                        pe.wait_ge(h2_act, g - 1)
                    for i in range(4):
                        k = 4 * kh + i
                        last = pe.transpose(PS[:, 6 + g % 2, i * P:(i + 1) * P], xr[:, t % 2, k * P:(k + 1) * P], ident[:])
                    last.then_inc(h2_pe, 1)

            for t in range(TT):
                rows = slice(t * P, (t + 1) * P)
                pe.wait_ge(yt_lo, 2 * KT - (4 if t < 4 else 0))
                for nh in range(2):
                    q = 2 * t + nh
                    cols = slice(nh * BANK, (nh + 1) * BANK)
                    if q >= 4:
                        pe.wait_ge(x1_ok, q - 3)
                    for k in range(KT):
                        if q == 0:
                            pe.wait_ge(w_ready, N_PROJ + k + 1)
                        hi, lo = wo[k][:, 0, :], wo[k][:, 1, :]
                        last = three(PS[:, q % 4, :], (yh[:, k, rows], yl[:, k, rows]), (hi[:, cols], lo[:, cols]),
                                     k == 0, k == KT - 1)
                    last.then_inc(op_pe, 1)
                if t >= 2:
                    turn2(t - 2)

            def gate_up(i, first=False):
                for a in range(2):
                    for j, done, freed in ((0, g_pe, silu_ok), (1, u_pe, mul_ok)):
                        slot = 2 * a + j
                        pe.wait_ge(w_ready, N_FFN0 + 6 * i + slot + 1)
                        for hf in range(2):
                            idx = 4 * i + 2 * a + hf
                            cols = slice(hf * BANK, (hf + 1) * BANK)
                            if first and a == 0:
                                if j == 0:
                                    if hf == 1:
                                        turn2(TT - 2)
                                        turn2(TT - 1)
                                    pe.wait_ge(x1_ok, 2 * TT)
                                    pe.wait_ge(h2_lo, TT * (hf + 1))
                            else:
                                pe.wait_ge(freed, idx - 1)
                            for k in range(KT):
                                w = slice(k * P, (k + 1) * P)
                                last = three(PS[:, 2 * j + hf, :], (wf[slot][:, 0, w], wf[slot][:, 1, w]),
                                             (yh[:, k, cols], yl[:, k, cols]), k == 0, k == KT - 1)
                            last.then_inc(done, 1)

            def down(i, par, slot, n_ready):
                pe.wait_ge(gu_ready, 4 * i + 4)
                pe.wait_ge(w_ready, n_ready)
                for r in range(16):
                    q = 16 * i + r
                    t, nh = divmod(r, 2)
                    rows = slice(t * P, (t + 1) * P)
                    cols = slice(nh * BANK, (nh + 1) * BANK)
                    pe.wait_ge(acc_ok, 16 + q - 3)
                    for a in range(2):
                        last = three(PS[:, 4 + r % 4, :], (guh[par][:, a, rows], gul[par][:, a, rows]),
                                     (wf[slot + a][:, 0, cols], wf[slot + a][:, 1, cols]), a == 0, a == 1)
                    last.then_inc(dn_pe, 1)

            pe.sem_inc(dn_pe, 16)
            gate_up(0, True)
            pe.wait_ge(h2_act, 2 * TT)
            with pe.Fori(1, FI, 2) as i0:
                for odd in range(2):
                    i = i0 + odd
                    gate_up(i)
                    down(i - 1, odd, 4, N_FFN0 + 6 * i + 6)
            down(FI - 1, (FI - 1) % 2, 0, N_FFN0 + 6 * FI + 2)


_INS = ['x', 'c', 'positions', 'ada_w', 'ada_b', 'norm_attn_g', 'w_in', 'b_forget', 'dsa_norm_g', 'fox_norm_g', 'w_out',
        'norm_ffn_g', 'w_gate', 'w_up', 'w_down', 'final_norm_g']


def kernel(**inputs):
    import numpy as _np
    import concourse.bacc as _bacc
    from concourse import mybir as _mybir
    from concourse.bass_utils import run_bass_kernel_spmd as _run

    nc = _bacc.Bacc("TRN2", target_bir_lowering=False, num_devices=1)
    arrays, args = {}, []
    for name in _INS:
        a = _np.ascontiguousarray(inputs[name])
        arrays[f"in_{name}_dram"] = a
        args.append(nc.dram_tensor(f"in_{name}_dram", a.shape, _mybir.dt.from_np(a.dtype), kind="ExternalInput").ap())
    args.append(nc.dram_tensor("out_dram", (1, SEQ, D), _mybir.dt.float32, kind="ExternalOutput").ap())
    build(nc, *args)
    r = _run(nc, [arrays], core_ids=[0])
    return r.results[0]["out_dram"]
```
